# Optimizing a Trainium2 kernel written in Bass

```python
import jax, jax.numpy as jnp
from jax import lax
import numpy as np

D_MODEL = 1024
BATCH = 1
SEQ = 256
DEPTH = 2

N_MEM = 256
EPS = 1e-6
NEG = -1e30

NSA_HEAD_DIM = 64
NSA_HEADS = (D_MODEL // 2) // NSA_HEAD_DIM
NSA_KV_GROUPS = 2
NSA_Q_WIDTH = NSA_HEADS * NSA_HEAD_DIM
NSA_KV_WIDTH = NSA_KV_GROUPS * NSA_HEAD_DIM
L_CMP = 32
D_CMP = 16
CMP_HIDDEN = 2 * NSA_HEAD_DIM
L_SLC = 64
N_SLC_SEL = 16
WINDOW = 512
Q_BLOCK = 128
FORCE_BONUS = 1.0e3
SGU_WIDTH = D_MODEL // 4
SGU_GROUPS = 4
SGU_CHUNK = 128
POOL_WIDTH = D_MODEL // 4
POOL_WINDOWS = (2, 4, 8, 16)
N_BRANCH = 3
IN_SPLITS = (NSA_Q_WIDTH, 6 * NSA_KV_WIDTH, 3 * NSA_HEADS, 2 * SGU_WIDTH, POOL_WIDTH, N_BRANCH * D_MODEL)
IN_WIDTH = NSA_Q_WIDTH + 6 * NSA_KV_WIDTH + 3 * NSA_HEADS + 2 * SGU_WIDTH + POOL_WIDTH + N_BRANCH * D_MODEL
XA_HEADS = 4
XA_HEAD_DIM = 128
XA_WIDTH = XA_HEADS * XA_HEAD_DIM
PEER_HEADS = 8
PEER_KEYS = 128
PEER_EXPERTS = PEER_KEYS * PEER_KEYS
PEER_QDIM = 128
PEER_TOPK = 16
PEER_BLOCK = 128

kernel_name = "hybrid_nsa_sgu_pool_peer_block"

def rms_norm(x, g):
    xf = x.astype(jnp.float32)
    y = xf * lax.rsqrt(jnp.mean(xf * xf, axis=-1, keepdims=True) + EPS)
    return (y * g).astype(x.dtype)

def layer_norm(x, g, b):
    xf = x.astype(jnp.float32)
    mu = jnp.mean(xf, axis=-1, keepdims=True)
    var = jnp.mean(jnp.square(xf - mu), axis=-1, keepdims=True)
    return ((xf - mu) * lax.rsqrt(var + EPS) * g + b).astype(x.dtype)

def masked_softmax(s, mask):
    s = jnp.where(mask, s.astype(jnp.float32), NEG)
    e = jnp.exp(s - jnp.max(s, axis=-1, keepdims=True)) * mask
    return e / jnp.maximum(jnp.sum(e, axis=-1, keepdims=True), 1e-30)

def nsa_attention(q, kv, gate_logits, q_norm, k_norm, cmp_pe, cmp_w1, cmp_w2):
    B, S, H, dk = q.shape
    G = NSA_KV_GROUPS
    R = H // G
    scale = dk ** -0.5
    q = rms_norm(q, q_norm)

    n_cmp = (S - L_CMP) // D_CMP + 1
    cmp_idx = np.arange(n_cmp)[:, None] * D_CMP + np.arange(L_CMP)[None, :]
    kv_raw = jnp.moveaxis(kv[:, :, 0:2], 2, 0)
    blocks = kv_raw[:, :, cmp_idx] + cmp_pe[:, None, None, :, None, :]
    hid = jax.nn.gelu(jnp.einsum('cbnlgd,clde->cbnge', blocks, cmp_w1))
    comp = jnp.einsum('cbnge,ced->cbngd', hid, cmp_w2)
    k_c = rms_norm(comp[0], k_norm[0])
    v_c = comp[1]
    cmp_end = jnp.asarray(np.arange(n_cmp) * D_CMP + L_CMP - 1)

    n_slc = S // L_SLC
    n_sel = min(N_SLC_SEL, n_slc)
    c0 = np.arange(n_cmp)[:, None] * D_CMP
    s0 = np.arange(n_slc)[None, :] * L_SLC
    overlap = np.minimum(c0 + L_CMP, s0 + L_SLC) - np.maximum(c0, s0)
    cmp_to_slc = jnp.asarray(np.maximum(overlap, 0) / D_CMP, dtype=jnp.float32)
    k_s = rms_norm(kv[:, :, 2], k_norm[1]).reshape(B, n_slc, L_SLC, G, dk).transpose(0, 3, 1, 2, 4)
    v_s = kv[:, :, 3].reshape(B, n_slc, L_SLC, G, dk).transpose(0, 3, 1, 2, 4)

    pad = ((0, 0), (WINDOW, 0), (0, 0), (0, 0))
    k_w = jnp.pad(rms_norm(kv[:, :, 4], k_norm[2]), pad)
    v_w = jnp.pad(kv[:, :, 5], pad)

    n_qb = S // Q_BLOCK
    q_blocks = q.reshape(B, n_qb, Q_BLOCK, G, R, dk).transpose(1, 0, 2, 3, 4, 5)
    g_blocks = jax.nn.sigmoid(gate_logits.astype(jnp.float32)).reshape(B, n_qb, Q_BLOCK, G, R, 3)
    g_blocks = g_blocks.transpose(1, 0, 2, 3, 4, 5)
    gather = jax.vmap(jax.vmap(lambda kb, i: kb[i]))

    def block(args):
        qb, qblk, gblk = args
        t = qb * Q_BLOCK + jnp.arange(Q_BLOCK)
        s = jnp.einsum('bqgrd,bngd->bgrqn', qblk, k_c) * scale
        p_c = masked_softmax(s, cmp_end[None, :] <= t[:, None])
        o_c = jnp.einsum('bgrqn,bngd->bqgrd', p_c.astype(v_c.dtype), v_c)
        imp = jnp.einsum('bgqn,nj->bgqj', jnp.sum(p_c, axis=2), cmp_to_slc)
        cur = t // L_SLC
        j = jnp.arange(n_slc)[None, :]
        forced = (j == 0) | (j == cur[:, None]) | (j == cur[:, None] - 1)
        sel_score = jnp.where(j <= cur[:, None], imp + FORCE_BONUS * forced, NEG)
        top_val, top_idx = lax.top_k(sel_score, n_sel)
        k_sel = gather(k_s, top_idx)
        v_sel = gather(v_s, top_idx)
        pos = top_idx[..., None] * L_SLC + jnp.arange(L_SLC)
        mask_s = (top_val[..., None] > 0.5 * NEG) & (pos <= t[:, None, None])
        s = jnp.einsum('bqgrd,bgqnld->bgrqnl', qblk, k_sel) * scale
        p_s = masked_softmax(s.reshape(B, G, R, Q_BLOCK, n_sel * L_SLC),
                             mask_s.reshape(B, G, 1, Q_BLOCK, n_sel * L_SLC)).reshape(s.shape)
        o_s = jnp.einsum('bgrqnl,bgqnld->bqgrd', p_s.astype(v_sel.dtype), v_sel)
        k_win = lax.dynamic_slice_in_dim(k_w, qb * Q_BLOCK, WINDOW + Q_BLOCK, axis=1)
        v_win = lax.dynamic_slice_in_dim(v_w, qb * Q_BLOCK, WINDOW + Q_BLOCK, axis=1)
        kpos = qb * Q_BLOCK - WINDOW + jnp.arange(WINDOW + Q_BLOCK)
        delta = t[:, None] - kpos[None, :]
        mask_w = (delta >= 0) & (delta < WINDOW) & (kpos[None, :] >= 0)
        s = jnp.einsum('bqgrd,bkgd->bgrqk', qblk, k_win) * scale
        p_w = masked_softmax(s, mask_w)
        o_w = jnp.einsum('bgrqk,bkgd->bqgrd', p_w.astype(v_win.dtype), v_win)
        o = (gblk[..., 0:1] * o_c + gblk[..., 1:2] * o_s + gblk[..., 2:3] * o_w)
        return o.astype(qblk.dtype)

    out = lax.map(block, (jnp.arange(n_qb), q_blocks, g_blocks))
    return out.transpose(1, 0, 2, 3, 4, 5).reshape(B, S, H * dk)

def spatial_gating(zg, ln_g, ln_b, w_s, b_s):
    B, S, _ = zg.shape
    zg = jax.nn.gelu(zg)
    u, v = jnp.split(zg, 2, axis=-1)
    v = layer_norm(v, ln_g, ln_b)
    n_ch = S // SGU_CHUNK
    v = v.reshape(B, n_ch, SGU_CHUNK, SGU_GROUPS, SGU_WIDTH // SGU_GROUPS)
    w = w_s * jnp.tril(jnp.ones((SGU_CHUNK, SGU_CHUNK), w_s.dtype))
    mixed = jnp.einsum('gts,bnsgc->bntgc', w, v) + b_s.T[:, :, None]
    return u * mixed.reshape(B, S, SGU_WIDTH)

def multiscale_pool(p, w_pool, scale):
    B, S, C = p.shape
    cg = C // len(POOL_WINDOWS)
    pf = p.astype(jnp.float32)
    csum = jnp.cumsum(pf, axis=1)
    csum_pad = jnp.pad(csum, ((0, 0), (1, 0), (0, 0)))
    pos = jnp.arange(S)
    outs = []
    for gi, w in enumerate(POOL_WINDOWS):
        sl = slice(gi * cg, (gi + 1) * cg)
        lower = jnp.pad(csum_pad[:, :S - w + 1, sl], ((0, 0), (w - 1, 0), (0, 0)))
        count = jnp.minimum(pos + 1, w).astype(jnp.float32)[None, :, None]
        outs.append((csum[:, :, sl] - lower) / count - pf[:, :, sl])
    d = jnp.stack(outs, axis=2)
    y = jnp.einsum('bsgc,gcd->bsgd', d, w_pool.astype(jnp.float32)).reshape(B, S, C) * scale
    return y.astype(p.dtype)

def memory_xattn(h, mem_h, wq, wk, wv, q_norm, k_norm, wo):
    B, S, _ = h.shape
    M = mem_h.shape[1]
    q = rms_norm((h @ wq).reshape(B, S, XA_HEADS, XA_HEAD_DIM), q_norm)
    k = rms_norm((mem_h @ wk).reshape(B, M, XA_HEADS, XA_HEAD_DIM), k_norm)
    v = (mem_h @ wv).reshape(B, M, XA_HEADS, XA_HEAD_DIM)
    s = jnp.einsum('bshd,bmhd->bhsm', q, k).astype(jnp.float32) * (XA_HEAD_DIM ** -0.5)
    p = jax.nn.softmax(s, axis=-1)
    o = jnp.einsum('bhsm,bmhd->bshd', p.astype(v.dtype), v).reshape(B, S, XA_WIDTH)
    return o @ wo

def peer_ffn(h, wq, keys1, keys2, u_tab, v_tab):
    B, S, D = h.shape
    half = PEER_QDIM // 2
    tokens = h.reshape(-1, PEER_BLOCK, D)

    def step(ht):
        T = ht.shape[0]
        q = (ht @ wq).reshape(T, PEER_HEADS, 2, half)
        s1 = jnp.einsum('thd,kd->thk', q[:, :, 0], keys1).astype(jnp.float32)
        s2 = jnp.einsum('thd,kd->thk', q[:, :, 1], keys2).astype(jnp.float32)
        v1, i1 = lax.top_k(s1, PEER_TOPK)
        v2, i2 = lax.top_k(s2, PEER_TOPK)
        cand = (v1[..., :, None] + v2[..., None, :]).reshape(T, PEER_HEADS, PEER_TOPK * PEER_TOPK)
        cv, ci = lax.top_k(cand, PEER_TOPK)
        a = jnp.take_along_axis(i1, ci // PEER_TOPK, axis=-1)
        b = jnp.take_along_axis(i2, ci % PEER_TOPK, axis=-1)
        e = a * PEER_KEYS + b
        g = jax.nn.softmax(cv, axis=-1)
        act = jax.nn.gelu(jnp.einsum('thkd,td->thk', u_tab[e], ht))
        return jnp.einsum('thk,thkd->td', (g * act).astype(ht.dtype), v_tab[e])

    return lax.map(step, tokens).reshape(B, S, D)

def setup_inputs(seed: int = 0) -> dict:
    key = jax.random.key(seed)
    ks = iter(jax.random.split(key, 40))
    f32 = jnp.float32
    L, D, dk = DEPTH, D_MODEL, NSA_HEAD_DIM
    cg = POOL_WIDTH // len(POOL_WINDOWS)

    def nrm(shape, scale):
        return jax.random.normal(next(ks), shape, f32) * scale

    def gain(shape):
        return 1.0 + 0.02 * jax.random.normal(next(ks), shape, f32)

    return {
        "x": nrm((BATCH, SEQ, D), 1.0),
        "mem": nrm((BATCH, N_MEM, D), 1.0),
        "mix_norm": gain((L, D)),
        "w_in": nrm((L, D, IN_WIDTH), D ** -0.5),
        "nsa_q_norm": gain((L, dk)),
        "nsa_k_norm": gain((L, 3, dk)),
        "cmp_pe": nrm((L, 2, L_CMP, dk), 0.5),
        "cmp_w1": nrm((L, 2, L_CMP, dk, CMP_HIDDEN), (L_CMP * dk) ** -0.5),
        "cmp_w2": nrm((L, 2, CMP_HIDDEN, dk), CMP_HIDDEN ** -0.5),
        "sgu_ln_g": gain((L, SGU_WIDTH)),
        "sgu_ln_b": nrm((L, SGU_WIDTH), 0.02),
        "sgu_w": nrm((L, SGU_GROUPS, SGU_CHUNK, SGU_CHUNK), SGU_CHUNK ** -0.5),
        "sgu_b": gain((L, SGU_GROUPS, SGU_CHUNK)),
        "pool_w": nrm((L, len(POOL_WINDOWS), cg, cg), cg ** -0.5),
        "pool_scale": gain((L, POOL_WIDTH)),
        "lift_a": nrm((L, NSA_Q_WIDTH, D), NSA_Q_WIDTH ** -0.5),
        "lift_b": nrm((L, SGU_WIDTH, D), SGU_WIDTH ** -0.5),
        "lift_c": nrm((L, POOL_WIDTH, D), POOL_WIDTH ** -0.5),
        "w_out": nrm((L, D, D), D ** -0.5),
        "xa_norm": gain((L, D)),
        "mem_norm": gain((L, D)),
        "xa_wq": nrm((L, D, XA_WIDTH), D ** -0.5),
        "xa_wk": nrm((L, D, XA_WIDTH), D ** -0.5),
        "xa_wv": nrm((L, D, XA_WIDTH), D ** -0.5),
        "xa_q_norm": gain((L, XA_HEAD_DIM)),
        "xa_k_norm": gain((L, XA_HEAD_DIM)),
        "xa_wo": nrm((L, XA_WIDTH, D), XA_WIDTH ** -0.5),
        "ffn_norm": gain((L, D)),
        "peer_wq": nrm((L, D, PEER_HEADS * PEER_QDIM), D ** -0.5),
        "peer_keys1": nrm((L, PEER_KEYS, PEER_QDIM // 2), (PEER_QDIM // 2) ** -0.5),
        "peer_keys2": nrm((L, PEER_KEYS, PEER_QDIM // 2), (PEER_QDIM // 2) ** -0.5),
        "peer_u": nrm((L, PEER_EXPERTS, D), D ** -0.5),
        "peer_v": nrm((L, PEER_EXPERTS, D), 0.25),
    }

def reference(x, mem, mix_norm, w_in, nsa_q_norm, nsa_k_norm, cmp_pe, cmp_w1, cmp_w2,
              sgu_ln_g, sgu_ln_b, sgu_w, sgu_b, pool_w, pool_scale, lift_a, lift_b, lift_c,
              w_out, xa_norm, mem_norm, xa_wq, xa_wk, xa_wv, xa_q_norm, xa_k_norm, xa_wo,
              ffn_norm, peer_wq, peer_keys1, peer_keys2, peer_u, peer_v):
    B, S, D = x.shape
    split_points = [int(c) for c in np.cumsum(IN_SPLITS)[:-1]]
    for l in range(DEPTH):
        h = rms_norm(x, mix_norm[l])
        z = h @ w_in[l]
        z_q, z_kv, z_g, z_sgu, z_pool, z_merge = jnp.split(z, split_points, axis=-1)
        o_a = nsa_attention(z_q.reshape(B, S, NSA_HEADS, NSA_HEAD_DIM),
                            z_kv.reshape(B, S, 6, NSA_KV_GROUPS, NSA_HEAD_DIM),
                            z_g.reshape(B, S, NSA_HEADS, 3),
                            nsa_q_norm[l], nsa_k_norm[l], cmp_pe[l], cmp_w1[l], cmp_w2[l])
        o_b = spatial_gating(z_sgu, sgu_ln_g[l], sgu_ln_b[l], sgu_w[l], sgu_b[l])
        o_c = multiscale_pool(z_pool, pool_w[l], pool_scale[l])
        gate = jax.nn.sigmoid(z_merge.astype(jnp.float32)).reshape(B, S, N_BRANCH, D).astype(x.dtype)
        merged = (gate[:, :, 0] * (o_a @ lift_a[l]) + gate[:, :, 1] * (o_b @ lift_b[l])
                  + gate[:, :, 2] * (o_c @ lift_c[l]))
        x = x + merged @ w_out[l]
        x = x + memory_xattn(rms_norm(x, xa_norm[l]), rms_norm(mem, mem_norm[l]),
                             xa_wq[l], xa_wk[l], xa_wv[l], xa_q_norm[l], xa_k_norm[l], xa_wo[l])
        x = x + peer_ffn(rms_norm(x, ffn_norm[l]), peer_wq[l], peer_keys1[l], peer_keys2[l],
                         peer_u[l], peer_v[l])
    return x


_drawn_inputs = setup_inputs


def setup_inputs(seed=0):
    import zlib

    import numpy as np

    out = dict(_drawn_inputs(seed))
    spreads = {}
    factors = {'nsa_q_norm': 7.905,
     'nsa_k_norm': 6.932,
     'sgu_ln_g': 4.647,
     'sgu_ln_b': 4.864,
     'sgu_b': 3.74,
     'pool_scale': 3.207,
     'xa_norm': 6.751,
     'mem_norm': 5.666,
     'xa_q_norm': 6.623,
     'xa_k_norm': 6.771,
     'ffn_norm': 3.818}
    for name, (base, spread) in spreads.items():
        noise = np.random.default_rng([zlib.crc32(name.encode()), seed]).standard_normal(out[name].shape)
        drawn = base * np.exp(spread * noise) if base else spread * noise
        out[name] = __import__('jax').numpy.asarray(drawn.astype(out[name].dtype))
    for name, factor in factors.items():
        out[name] = (out[name] * factor).astype(out[name].dtype)
    return out
```

```python
from contextlib import ExitStack

import numpy as np
import concourse.bass as bass
from concourse import mybir

F32 = mybir.dt.float32
F32R = mybir.dt.float32r
BF16 = mybir.dt.bfloat16
U32 = mybir.dt.uint32
ALU = mybir.AluOpType
ACT = mybir.ActivationFunctionType
AX = mybir.AxisListType

P = 128
DEPTH, D, S, MEM = 2, 1024, 256, 256
EPS, NEG = 1e-6, -1e30
HEADS, DK, KVG = 8, 64, 2
PAIRS = HEADS // 2
L_CMP, D_CMP, CMP_HID = 32, 16, 128
N_CMP = (S - L_CMP) // D_CMP + 1
NP_ = 16
SGU_W, SGU_G, POOL_W = 256, 4, 256
WINDOWS = (2, 4, 8, 16)
XH, XD = 4, 128
PH, KEYS, TOPK = 8, 128, 16
EXPERTS = KEYS * KEYS
T = S // P
KD = D // P
COL = 512
LOWEST = -3.0e38

PER_CHUNK = 4
SLOTS = 4
RAW = 2
HELD = RAW * PER_CHUNK
BLOCKS = (["mem_k", "mem_v", "z_q", "z_kv0", "z_kv1", "z_sgu"] + [f"z_m{i}" for i in range(6)]
          + ["lift_a0", "lift_b0", "lift_c0", "lift_a1", "lift_b1", "lift_c1"]
          + ["out0", "out1", "xq", "xo0", "xo1", "pq0", "pq1"])
DEPTH_OF = {"lift_a": 4, "lift_b": 2, "lift_c": 2, "xo": 4}


def pieces_of(block):
    return DEPTH_OF.get(block.rstrip("01"), KD)


FIRST = {}
_n = 0
for _b in BLOCKS:
    FIRST[_b] = _n
    _n += pieces_of(_b)
PROJ = _n
U_PIECES = V_PIECES = KEYS * 2
PIECES = PROJ + U_PIECES + V_PIECES
CHUNKS = PIECES // PER_CHUNK
LAST = {b: FIRST[b] + pieces_of(b) for b in BLOCKS}
PARITY = {b: i % 2 for i, b in enumerate(BLOCKS)}
assert PROJ % (2 * PER_CHUNK) == 0

USES = [(f"mem_T{i}", i) for i in range(4)] + [(f"mix_T{i}", i) for i in range(4)]
USES += [("mk_T0", 0), ("mk_T1", 1), ("zg", 2), ("raw_T0", 0), ("raw_T1", 1), ("kn_T0", 2), ("kn_T1", 3),
         ("q_T0", 0), ("q_T1", 1), ("hid", 2), ("pool_d0", 0), ("pool_d1", 1), ("cmp_k", 2), ("cmp_v", 3),
         ("mixed", 0), ("pool_y", 1), ("kc_T", 2), ("cmp_s", 3)]
UNITS = [(t, br, j) for t in range(T) for br in range(2) for j in range(PAIRS)]
USES += [("s0", 0), ("s1", 1)]
for _u in range(len(UNITS)):
    USES += [(f"p_T{_u}", 2)]
    if _u + 2 < len(UNITS):
        USES += [(f"s{_u + 2}", _u % 2)]
    if _u % PAIRS == 0:
        USES += [(f"o{_u // PAIRS}", 3)]
USES += [("pc_T", 0), ("oc0", 1), ("oc1", 2), ("br_T0", 3), ("br_T1", 0), ("br_T2", 1)]
USES += [(f"mg_T{i}", i) for i in range(4)] + [(f"xa_T{i}", i) for i in range(4)]
USES += [("xq_T0", 0), ("xq_T1", 1)]
XUNITS = [(t, j) for t in range(T) for j in range(XH // 2)]
USES += [("xs0", 0), ("xs1", 1)]
for _u in range(len(XUNITS)):
    USES += [(f"xp_T{_u}", 2)]
    if _u + 2 < len(XUNITS):
        USES += [(f"xs{_u + 2}", _u % 2)]
    if _u % 2 == 0:
        USES += [(f"xo_{_u // 2}", 3)]
USES += [("xo_T0", 0), ("xo_T1", 1)]
USES += [(f"ff_T{i}", i) for i in range(4)] + [(f"pq_T{i}", i) for i in range(4)]
USES += [(f"ps0_{i}", i) for i in range(4)] + [(f"ps1_{i}", i) for i in range(4)]
USES += [("slot_T0", 0), ("slot_T1", 1)]
G_TOK = 4
G_STEPS = S // G_TOK
HALF = KEYS // 2
PARTS = 3
HOT = KEYS + PARTS * HALF
assert G_STEPS == HALF

C_MIX, C_XA, C_FFN, C_MEM = 0, 8, 16, 24
C_QN, C_KN, C_XQN, C_XKN, C_PSC, C_SB, C_END = 32, 33, 36, 37, 38, 40, 44
K_ID, K_IO, K_CM, K_CN, K_C1, K_BM, K_I16 = 0, 128, 256, 512, 544, 576, 584
K_END = K_I16 + 16 + 1

OWN = [("memx", T * D), ("xn", T * D), ("mk", T * 512), ("mv", T * 512), ("mkT", XH * MEM), ("zkv", T * 768),
       ("zp", T * POOL_W), ("gates", T * 3072), ("ng", T * 24), ("knd", T * 512), ("KV2", 4 * S), ("blk", 2 * 16 * 32),
       ("w1", 4096), ("w2", 128), ("pe", 32), ("kTm", 2 * 4 * S), ("qT", PAIRS * S), ("ob", T * SGU_W),
       ("vn", T * SGU_W), ("sgw", 512), ("pw", 512), ("keys", 256), ("lnrow", 512), ("zgw", 192), ("tril", 128),
       ("pm", 1536), ("tmp", T * 512), ("cmp", 1024)]
REUSE = {"zq": ("memx", 0), "sg": ("memx", 1024), "rawd": ("mk", 0), "dT": ("mk", 0), "o": ("knd", 0),
         "junk": ("kTm", 0), "merged": ("w1", 0), "xo": ("gates", 4096), "pq": ("gates", 0), "pqT": ("gates", 2048),
         "sring": ("KV2", 0), "pT": ("blk", 0), "yT": ("vn", 0), "vblk": ("lnrow", 0)}
OFF = {}
_o = 0
for _name, _size in OWN:
    OFF[_name] = _o
    _o += _size
for _name, (_first, _in) in REUSE.items():
    OFF[_name] = OFF[_first] + _in
BIG = KEYS * S
assert _o <= BIG, _o


class Signal:

    def __init__(self, sem, per, primed=0):
        self.sem, self.per, self.primed, self.sent = sem, per, primed, 0

    def value(self, layer, k):
        return layer * self.per + (k + self.primed)


def stream_slot(n):
    return n % SLOTS


def trunk(nc, x, mem, stream, cols, parb, parr, lnrow, zgw, consts, pm, tril, out):
    ctx = ExitStack()
    with ctx:
        def sb(name, shape, dt=F32):
            return ctx.enter_context(nc.sbuf_tensor(name, shape, dt))

        def sem(name):
            return ctx.enter_context(nc.semaphore(name))

        raw = sb("raw", [P, RAW, PER_CHUNK, COL])
        w_hi = sb("w_hi", [P, SLOTS, COL], F32R)
        w_lo = sb("w_lo", [P, SLOTS, COL], F32R)
        X = sb("X", [P, T, D])
        h_hi = sb("h_hi", [P, KD, S], F32R)
        h_lo = sb("h_lo", [P, KD, S], F32R)
        big = sb("big", [P, BIG])
        eg = sb("eg", [P, 2, 2, S], F32R)
        cst = sb("cst", [P, K_END])
        col = sb("col", [P, C_END])
        zg_hi = sb("zg_hi", [P, KD, 24], F32R)
        zg_lo = sb("zg_lo", [P, KD, 24], F32R)
        zeros = sb("zeros", [P, 128], BF16)
        iota_b = sb("iota_b", [P, P], BF16)
        rout = sb("rout", [P, 2048])
        topv = sb("topv", [P, PH * 2 * 16])
        topi = sb("topi", [P, PH * 2 * 16], U32)
        topf = sb("topf", [P, PH * 2 * 16])
        cv = sb("cv", [P, T, PH, TOPK])
        ab = sb("ab", [P, 2, T, PH, TOPK])
        st = sb("st", [P, 96])
        tblw = cst[:, K_END - 1:K_END]

        def region(name, size, *dims):
            v = big[:, OFF[name]:OFF[name] + size]
            if not dims:
                return v
            names = "abcde"[:len(dims)]
            return v.rearrange(f"p ({' '.join(names)}) -> p {' '.join(names)}", **dict(zip(names[1:], dims[1:])))

        memx, xn, junk = (region(n, T * D, T, D) for n in ("memx", "xn", "junk"))
        mk, mv, zq, sg, ot, xo, tmp = (region(n, T * 512, T, 512) for n in ("mk", "mv", "zq", "sg", "o", "xo", "tmp"))
        mkT = region("mkT", XH * MEM, XH, MEM)
        zkv = region("zkv", T * 768, T, 6, 128)
        zp = region("zp", T * POOL_W, T, POOL_W)
        gates = region("gates", T * 3072, T, 3072)
        ng = region("ng", T * 24, T, 24)
        rawd = region("rawd", T * 512, T, 4, 2, DK)
        knd = region("knd", T * 512, T, 2, KVG, 2, DK)
        KV2 = region("KV2", 4 * S, 4, S)
        blk = region("blk", 1024, 2, 16, 2, 16)
        w1 = region("w1", 4096, 2, 16, 128)
        w2 = region("w2", 128, 2, DK)
        pe = region("pe", 32, 2, 16)
        kTm = region("kTm", 2 * 4 * S, 2, KVG, 2, S)
        qT = region("qT", PAIRS * S, PAIRS, S)
        sring = region("sring", 1024, 2, 2, 256)
        pT = region("pT", 1024, 2, 4, 128)
        vblk = region("vblk", 512)
        ob, vn = (region(n, T * SGU_W, T, SGU_W) for n in ("ob", "vn"))
        dT = region("dT", T * 512, T, 4, P)
        yT = region("yT", 512, 2, S)
        sgw = region("sgw", 512, SGU_G, P)
        pw = region("pw", 512, 4, P)
        keys = region("keys", 256)
        lnr = region("lnrow", 512)
        zgr = region("zgw", 192, KD, 24)
        trl = region("tril", 128)
        pmx = region("pm", 1536, 3, 4, P)
        merged = region("merged", T * D, T, D)
        pq = region("pq", T * D, T, D)
        pqT = region("pqT", PH * S, PH, S)
        cm = big[:, OFF["cmp"]:OFF["cmp"] + 1024]
        hidT = cm[:, 0:64].rearrange("p (c g n) -> p c g n", c=2, g=2)
        hid_rep = cm[:, 64:192].rearrange("p (g r n) -> p g r n", g=2, r=4)
        kcs = cm[:, 192:256]
        kcq = cm[:, 256:320]
        kcd = cm[:, 320:448].rearrange("p (a d) -> p a d", a=2)
        KcB = cm[:, 448:512].rearrange("p (g h n) -> p g h n", g=2, h=2)
        sc = cm[:, 512:768].rearrange("p (t h n) -> p t h n", t=2, h=8)
        pcT = cm[:, 768:1024].rearrange("p (t s) -> p t s", t=2)
        xqt, xqT = zq, region("qT", XH * S, XH, S)
        experts = big[:, :].rearrange("p (a t) -> p a t", t=S)

        ident = cst[:, K_ID:K_ID + P]
        iota = cst[:, K_IO:K_IO + P]
        cmask = cst[:, K_CM:K_CM + 256]
        cneg = cst[:, K_CN:K_CN + 32].rearrange("p (t n) -> p t n", t=2)
        cone = cst[:, K_C1:K_C1 + 32].rearrange("p (t n) -> p t n", t=2)
        bmask = cst[:, K_BM:K_BM + 8]
        iota16 = cst[:, K_I16:K_I16 + 16]

        rs = rout[:, :].rearrange("p (h f k) -> p h f k", h=PH, f=2)
        cand = rout[:, :].rearrange("p (h i j) -> p h i j", h=PH, i=TOPK)
        onehot = rout[:, :].rearrange("p (m j) -> p m j", j=TOPK)
        hots = rout[:, 0:HOT * G_TOK].bitcast(BF16).rearrange("p (s r k) -> p s r k", s=2, r=G_TOK)
        slot_a, slot_b = topv, topf
        slot_w = cv[:, :, :, :].rearrange("p t h k -> p (t h k)")
        slot_parts = ab[:, :, :, :, :].rearrange("p w t h k -> p (w t h k)").bitcast(BF16)[:, 0:PARTS * S].rearrange(
            "p (c t) -> p c t", c=PARTS)
        tv = topv[:, :].rearrange("p (h f k) -> p h f k", h=PH, f=2)
        ti = topi[:, :].rearrange("p (h f k) -> p h f k", h=PH, f=2)
        tf = topf[:, :].rearrange("p (h f k) -> p h f k", h=PH, f=2)
        iab = topv[:, :].rearrange("p (w m) -> p w m", w=2)
        ci = topi[:, 0:128]
        cia = topi[:, 128:256]

        ssx = st[:, 0:4]
        ssh = st[:, 4:28]
        coef = st[:, 28:36]
        nmx = st[:, 36:40].rearrange("p (r h) -> p r h", r=2)
        bns = st[:, 40:52].rearrange("p (t s) -> p t s", t=2)
        mvr = st[:, 52:56].rearrange("p (t s) -> p t s", t=2)
        ssk = st[:, 56:57]
        cmx = st[:, 58:74]
        sums = st[:, 74:90].rearrange("p (r h) -> p r h", r=2)

        acc = ctx.enter_context(nc.psum_tensor("acc", [P, 4, COL], F32))
        aux = ctx.enter_context(nc.psum_tensor("aux", [P, 4, COL], F32))

        chunk_in = [sem(f"chunk_in{r}") for r in range(RAW)]
        hi_ready = sem("hi_ready")
        lo_ready = sem("lo_ready")
        used = sem("used")

        PER = dict(
            layer_free=1,
            mem_in=32, params=16 * 6,
            x_sq=3, x_mean=3, x_sqrt=3, mem_n=1, xn_ready=3,
            hi_T=26, h_ready=7,
            mk_mean=1, mk_sqrt=1, mk_n=1,
            zg_split=1, rawd_ready=1, qk_mean=1, qk_sqrt=1, knd_ready=1, qn_ready=1, blk_ready=1,
            hidrep=1, kc_mean=1, kc_sqrt=1, kcd_ready=1,
            sgw_ready=1, ln_mean=1, ln_sqrt=1, vn_ready=1, ob_ready=1,
            cs_ready=1, cs_exp=1, pc_ready=1,
            s_ready=len(UNITS), p_exp=len(UNITS), o_ready=1, merged_ready=1,
            xq_mean=1, xq_sqrt=1, xq_n=1, xs_ready=len(XUNITS), xo_ready=1,
            cv_ready=1, w_exp=1, w_ready=1,
            u_out=KEYS, hot_ready=4 * S, g_full=2 * G_STEPS, g_out=2 * G_STEPS,
            eg_hi=KEYS, eg_ready=KEYS, v_out=1,
            acc_free0=sum(v == 0 for v in PARITY.values()), acc_free1=sum(v == 1 for v in PARITY.values()))
        PRIMED = dict(layer_free=1, u_out=4, g_out=2, acc_free0=1, acc_free1=1)
        sig = {n: Signal(sem(n), per, PRIMED.get(n, 0)) for n, per in PER.items()}
        n_uses = [sum(b == k for _, b in USES) for k in range(4)]
        filled = [Signal(sem(f"aux{b}_filled"), n_uses[b]) for b in range(4)]
        drained = [Signal(sem(f"aux{b}_drained"), n_uses[b], 1) for b in range(4)]
        turn, seen = {}, [0] * 4
        for name, b in USES:
            turn[name] = (b, seen[b])
            seen[b] += 1
        dve_step = sem("dve_step")
        act_step = sem("act_step")
        x_in = sem("x_in")
        const_in = sem("const_in")
        zero_set = sem("zero_set")
        settled = sem("settled")
        out_done = sem("out_done")

        def bank(name):
            return aux[:, turn[name][0], :]

        class Engine:

            def __init__(self, eng, layer, own=None):
                self.e, self.layer, self.own, self.n = eng, layer, own, 0

            def wait(self, name, k=None):
                s = sig[name]
                self.e.wait_ge(s.sem, s.value(self.layer, s.per if k is None else k))

            def wait_filled(self, use):
                b, j = turn[use]
                self.e.wait_ge(filled[b].sem, filled[b].value(self.layer, j + 1))

            def wait_drained(self, use):
                b, j = turn[use]
                self.e.wait_ge(drained[b].sem, drained[b].value(self.layer, j + 1))

            def wait_bank_free(self, use):
                b, j = turn[use]
                self.e.wait_ge(drained[b].sem, drained[b].value(self.layer, j))

            def wait_block(self, block):
                i = BLOCKS.index(block)
                s = sig[f"acc_free{i % 2}"]
                self.e.wait_ge(s.sem, s.value(self.layer, i // 2 + 1))

            def wait_pieces(self, n):
                self.e.wait_ge(used, self.layer * PIECES + (SLOTS + n))

            def settle(self):
                self.e.sem_inc(settled, 1)

            def step(self, ins, name=None, drains=None, block=None):
                if drains is not None:
                    b, j = turn[drains]
                    ins.then_inc(drained[b].sem, 1)
                    drained[b].sent += 1
                    self.wait_drained(drains)
                elif block is not None:
                    s = sig[f"acc_free{BLOCKS.index(block) % 2}"]
                    ins.then_inc(s.sem, 1)
                    s.sent += 1
                    self.wait_block(block)
                elif name is not None:
                    s = sig[name]
                    ins.then_inc(s.sem, 1)
                    s.sent += 1
                    self.e.wait_ge(s.sem, s.value(self.layer, s.sent))
                else:
                    self.n += 1
                    ins.then_inc(self.own, 1)
                    self.e.wait_ge(self.own, self.n)

        block = ctx.enter_context(nc.Block())

        @block.sync
        def _(sp):
            sp.dma_start(X[:], x.rearrange("(t p) d -> p t d", p=P)).then_inc(x_in, 16)
            with sp.Fori(0, DEPTH * CHUNKS // RAW) as i:
                for r in range(RAW):
                    sp.wait_ge(lo_ready, i * (RAW * PER_CHUNK) + (r + 1) * PER_CHUNK)
                    sp.dma_start(raw[:, r], stream[bass.ds(i * RAW + r, 1)].rearrange(
                        "o p (k c) -> p (o k) c", c=COL)).then_inc(chunk_in[r], 16)
            sp.wait_ge(sig["layer_free"].sem, 1 + DEPTH)
            sp.dma_start(out.rearrange("(t p) d -> p t d", p=P), X[:]).then_inc(out_done, 16)
            sp.wait_ge(out_done, 16)

        @block.gpsimd
        def _(pool):
            pool.sem_inc(lo_ready, HELD)
            with pool.Fori(0, DEPTH * PIECES // (RAW * PER_CHUNK)) as i:
                for k in range(RAW * PER_CHUNK):
                    pool.wait_ge(hi_ready, i * (RAW * PER_CHUNK) + (k + 1))
                    pool.wait_ge(used, i * (RAW * PER_CHUNK) + (k + 1))
                    nc.gpsimd.tensor_tensor(w_lo[:, k % SLOTS, :], raw[:, k // PER_CHUNK, k % PER_CHUNK, :],
                                            w_hi[:, k % SLOTS, :].bitcast(F32), ALU.subtract).then_inc(lo_ready, 1)

        @block.scalar
        def _(act):
            act.dma_start(cst[:], consts).then_inc(const_in, 16)
            with act.Fori(0, DEPTH) as layer:
                a = Engine(act, layer, act_step)
                done = [0]

                PER_TURN = RAW * PER_CHUNK
                TURNS = CHUNKS // RAW * 16

                def hi_piece(k, turn_value, free_value):
                    act.wait_ge(chunk_in[(k // PER_CHUNK) % RAW], turn_value)
                    act.wait_ge(used, free_value)
                    nc.scalar.activation(w_hi[:, k % SLOTS, :], raw[:, (k // PER_CHUNK) % RAW, k % PER_CHUNK, :],
                                         ACT.Copy).then_inc(hi_ready, 1)

                def hi(n):
                    for _ in range(n):
                        k = done[0]
                        hi_piece(k, layer * TURNS + (k // PER_TURN + 1) * 16, layer * PIECES + (k + 1))
                        done[0] += 1
                        for m in range(6):
                            if done[0] == LAST[f"z_m{m}"] + SLOTS:
                                read_gates(m)

                def read_gates(m):
                    b = f"z_m{m}"
                    a.wait_pieces(LAST[b])
                    for t in range(T):
                        a.step(nc.scalar.activation(gates[:, t, m * COL:(m + 1) * COL], acc[:, PARITY[b] * 2 + t, :],
                                                    ACT.Sigmoid), block=b if t == T - 1 else None)

                def hi_T(name, k0, nk, gain=None):
                    a.wait_filled(name)
                    src = bank(name).rearrange("p (k t) -> p k t", t=S)
                    for k in range(nk):
                        scale = 1.0 if gain is None else col[:, gain + k:gain + k + 1]
                        a.step(nc.scalar.activation(h_hi[:, k0 + k, :], src[:, k, :], ACT.Copy, scale=scale),
                               "hi_T" if k == nk - 1 else None)

                def squares(srcs, first):
                    for n, src in enumerate(srcs):
                        a.step(nc.scalar.activation(junk[:, n % 2, :], src, ACT.Square,
                                                    accum_out=ssx[:, first + n:first + n + 1]),
                               "x_sq" if n == len(srcs) - 1 else None)

                def root(v, mean, done_name, k=1):
                    a.wait(mean, k)
                    a.step(nc.scalar.activation(v, v, ACT.Sqrt), done_name)

                hi(SLOTS)
                a.wait("layer_free", 0)
                for dst, src in ((col[:], cols), (memx, None)):
                    src = mem.rearrange("(t p) d -> p t d", p=P) if src is None else \
                        src[bass.ds(layer, 1)].rearrange("o p c -> p (o c)")
                    act.dma_start(dst, src).then_inc(sig["mem_in"].sem, 16)
                for name, size, src in (("w1", 4256, parb), ("sgw", 1280, parr), ("zgw", 192, zgw)):
                    act.dma_start(big[:, OFF[name]:OFF[name] + size],
                                  src[bass.ds(layer, 1)].rearrange("o p c -> p (o c)")).then_inc(sig["params"].sem, 16)
                act.dma_start(lnr, lnrow[bass.ds(layer, 1)].broadcast_to((P, 512))).then_inc(sig["params"].sem, 16)
                act.dma_start(trl, tril).then_inc(sig["params"].sem, 16)
                act.dma_start(big[:, OFF["pm"]:OFF["pm"] + 1536], pm).then_inc(sig["params"].sem, 16)

                a.wait("mem_in")
                squares([memx[:, 0, :], memx[:, 1, :], X[:, 0, :], X[:, 1, :]], 0)
                root(ssx, "x_mean", "x_sqrt", 1)
                for i in range(4):
                    hi_T(f"mem_T{i}", 2 * i, 2, C_MEM + 2 * i)
                hi(16)
                for i in range(4):
                    hi_T(f"mix_T{i}", 2 * i, 2, C_MIX + 2 * i)
                root(ssh[:, 0:8], "mk_mean", "mk_sqrt")
                hi(32)
                root(ssh, "qk_mean", "qk_sqrt")
                a.wait_pieces(LAST["z_sgu"])
                for t in range(T):
                    a.step(nc.scalar.activation(sg[:, t, :], acc[:, PARITY["z_sgu"] * 2 + t, :], ACT.Gelu_apprx_tanh),
                           block="z_sgu" if t == T - 1 else None)
                a.wait_filled("zg")
                a.step(nc.scalar.activation(ng, bank("zg")[:, 0:48].rearrange("p (t c) -> p t c", t=T), ACT.Sigmoid),
                       drains="zg")
                root(mvr[:, :, 1], "ln_mean", "ln_sqrt")
                hi(6)
                a.wait_filled("hid")
                a.step(nc.scalar.activation(hidT[:, :, :, 0:N_CMP], bank("hid")[:, 0:64].rearrange(
                    "p (c g n) -> p c g n", c=2, g=2)[:, :, :, 0:N_CMP], ACT.Gelu_apprx_tanh), drains="hid")
                hi(3)
                a.wait("kc_mean")
                a.step(nc.scalar.activation(ssk[0:32], ssk[0:32], ACT.Sqrt), "kc_sqrt")
                hi(7)
                a.wait("cs_ready")
                a.step(nc.scalar.activation(sc, sc, ACT.Exp), "cs_exp")
                for u, (t, br, j) in enumerate(UNITS):
                    w = P * (t + 1)
                    a.wait("s_ready", u + 1)
                    for h in range(2):
                        a.step(nc.scalar.activation(sring[:, u % 2, h, 0:w], sring[:, u % 2, h, 0:w], ACT.Exp,
                                                    bias=nmx[:, u % 2, h:h + 1],
                                                    accum_out=sums[:, (t * 2 + br) % 2, 2 * j + h:2 * j + h + 1]),
                               "p_exp" if h == 1 else None)
                    hi(2)
                for i in range(3):
                    hi_T(f"br_T{i}", 2 * i, 2)
                for k in range(2):
                    a.step(nc.scalar.activation(h_hi[:, 6 + k, :], yT[:, k, :], ACT.Copy), "hi_T" if k else None)
                hi(16)
                for i in range(4):
                    hi_T(f"mg_T{i}", 2 * i, 2)
                hi(16)
                a.wait_block("out1")
                squares([X[:, 0, :], X[:, 1, :]], 2)
                root(ssx[:, 2:4], "x_mean", "x_sqrt", 2)
                for i in range(4):
                    hi_T(f"xa_T{i}", 2 * i, 2, C_XA + 2 * i)
                hi(8)
                root(ssh[:, 0:8], "xq_mean", "xq_sqrt")
                for u, (t, j) in enumerate(XUNITS):
                    a.wait("xs_ready", u + 1)
                    for h in range(2):
                        a.step(nc.scalar.activation(sring[:, u % 2, h, :], bank(f"xs{u}")[:, h * MEM:(h + 1) * MEM],
                                                    ACT.Exp, scale=XD ** -0.5, bias=nmx[:, u % 2, h:h + 1],
                                                    accum_out=sums[:, t, 2 * j + h:2 * j + h + 1]),
                               **(dict(drains=f"xs{u}") if h else {}))
                for i in range(2):
                    hi_T(f"xo_T{i}", 2 * i, 2)
                hi(8)
                a.wait_block("xo1")
                squares([X[:, 0, :], X[:, 1, :]], 2)
                root(ssx[:, 2:4], "x_mean", "x_sqrt", 3)
                for i in range(4):
                    hi_T(f"ff_T{i}", 2 * i, 2, C_FFN + 2 * i)
                hi(16)
                assert done[0] == PROJ + SLOTS
                def key_rows(i, key):
                    at = slice(key, key + 1) if isinstance(i, int) else bass.ds(i * 4 + key, 1)
                    return experts[:, at, :].rearrange("p o t -> p (o t)")

                def key_out(i, key):
                    act.wait_ge(used, layer * PIECES + i * 8 + (PROJ + SLOTS + 2 * (key + 1)))
                    nc.scalar.activation(key_rows(i, key), acc[:, key % 4, 0:S],
                                         ACT.Gelu_apprx_tanh).then_inc(sig["u_out"].sem, 1)

                for half in range(2):
                    a.step(nc.scalar.activation(tblw, tblw, ACT.Gelu_apprx_tanh))
                    hi(2)
                    with act.Fori(0, HALF // 4 - 1) as i:
                        for q in range(4):
                            key_out(i, half * HALF + q)
                            for r in range(2):
                                k = done[0] + 2 * q + r
                                hi_piece(k, layer * TURNS + i * 16 + (k // PER_TURN + 1) * 16,
                                         layer * PIECES + i * 8 + (k + 1))
                    done[0] += 2 * HALF - 8
                    for q in range(4):
                        key_out(0, half * HALF + HALF - 4 + q)
                        if q < 3:
                            hi(2)
                    if half == 0:
                        a.wait("cv_ready")
                        a.step(nc.scalar.activation(slot_w, slot_w, ACT.Exp), "w_exp")
                sig["u_out"].sent += KEYS
                def key_hi(i, key):
                    act.wait_ge(used, layer * PIECES + i * 8 + (SLOTS + PROJ + U_PIECES + 2 * (key - 1)))
                    nc.scalar.activation(eg[:, key % 2, 0, :], key_rows(i, key), ACT.Copy).then_inc(sig["eg_hi"].sem, 1)

                a.wait("g_out", G_STEPS)
                key_hi(0, 0)
                key_hi(0, 1)
                key = 2
                for steps, peeled in ((HALF // 4 - 1, 2), (HALF // 4, 0)):
                    with act.Fori(0, steps) as i:
                        for q in range(4):
                            for r in range(2):
                                k = done[0] + 2 * q + r
                                hi_piece(k, layer * TURNS + i * 16 + (k // PER_TURN + 1) * 16,
                                         layer * PIECES + i * 8 + (k + 1))
                                if r == 0:
                                    key_hi(i, key + q)
                    done[0] += 8 * steps
                    key += 4 * steps
                    for _ in range(peeled):
                        hi(1)
                        key_hi(0, key)
                        hi(1)
                        key += 1
                    if key == HALF:
                        a.wait("g_out")
                        a.settle()
                assert key == KEYS and done[0] == PIECES
                a.settle()
                act.sem_clear(act_step)

        @block.tensor
        def _(pe_):
            pe_.sem_inc(used, SLOTS)
            pe_.wait_ge(const_in, 16)
            with pe_.Fori(0, DEPTH) as layer:
                e = Engine(pe_, layer)
                done = [0]
                hcount = [0]

                def fill(ins, use):
                    b, _ = turn[use]
                    ins.then_inc(filled[b].sem, 1)
                    filled[b].sent += 1

                def transposes(use, sources, waited=False):
                    if not waited:
                        e.wait_bank_free(use)
                    at = 0
                    for src in sources:
                        rows = src.shape[0]
                        ins = pe_.transpose(bank(use)[:, at:at + rows], src, ident[0:rows, 0:rows])
                        at += rows
                    fill(ins, use)

                def rows_T(uses, src):
                    for i, use in enumerate(uses):
                        transposes(use, [src[:, t, k * P:(k + 1) * P] for k in (2 * i, 2 * i + 1) for t in range(T)])

                piece_block = [(b, k, LAST[b] - FIRST[b]) for b in BLOCKS for k in range(pieces_of(b))]
                rows_of = {"lift_b": 4, "lift_c": 6}

                def take(n):
                    for _ in range(n):
                        b, k, depth = piece_block[done[0]]
                        if k == 0:
                            i = BLOCKS.index(b)
                            s = sig[f"acc_free{i % 2}"]
                            pe_.wait_ge(s.sem, s.value(layer, i // 2))
                        pe_.wait_ge(lo_ready, layer * PIECES + (HELD + done[0] + 1))
                        slot = done[0] % SLOTS
                        kt = rows_of.get(b.rstrip("01"), 0) + k
                        for t in range(T):
                            dst = acc[:, PARITY[b] * 2 + t, :]
                            ts = slice(t * P, (t + 1) * P)
                            pe_.matmul(dst, h_hi[:, kt, ts], w_hi[:, slot, :], start=(k == 0), stop=False)
                            pe_.matmul(dst, h_hi[:, kt, ts], w_lo[:, slot, :], start=False, stop=False)
                            ins = pe_.matmul(dst, h_lo[:, kt, ts], w_hi[:, slot, :], start=False, stop=(k == depth - 1))
                        ins.then_inc(used, 1)
                        done[0] += 1

                def rows_ready():
                    hcount[0] += 1
                    e.wait("h_ready", hcount[0])

                e.wait("layer_free", 0)
                e.wait("mem_n")
                rows_T([f"mem_T{i}" for i in range(4)], memx)
                rows_ready()
                take(16)
                e.wait("xn_ready", 1)
                rows_T([f"mix_T{i}" for i in range(4)], xn)
                rows_ready()
                take(16)
                e.wait("mk_n")
                for i in range(2):
                    transposes(f"mk_T{i}", [mk[:, t, h * XD:(h + 1) * XD] for h in (2 * i, 2 * i + 1) for t in range(T)])
                take(16)
                e.wait("zg_split")
                e.wait_bank_free("zg")
                for t in range(T):
                    for k in range(KD):
                        ts = slice(t * P, (t + 1) * P)
                        dst = bank("zg")[:, t * 24:(t + 1) * 24]
                        pe_.matmul(dst, h_hi[:, k, ts], zg_hi[:, k, :], start=(k == 0), stop=False)
                        pe_.matmul(dst, h_hi[:, k, ts], zg_lo[:, k, :], start=False, stop=False)
                        ins = pe_.matmul(dst, h_lo[:, k, ts], zg_hi[:, k, :], start=False, stop=(k == KD - 1))
                fill(ins, "zg")
                e.wait("rawd_ready")
                for i in range(2):
                    transposes(f"raw_T{i}", [rawd[:, t, cg, :, :] for cg in (2 * i, 2 * i + 1) for t in range(T)])
                e.wait("knd_ready")
                for br in range(2):
                    transposes(f"kn_T{br}", [knd[:, t, br, g, :, :] for g in range(KVG) for t in range(T)])
                take(3)
                e.wait("qn_ready")
                for i in range(2):
                    transposes(f"q_T{i}", [zq[:, t, j * P:(j + 1) * P] for j in (2 * i, 2 * i + 1) for t in range(T)])
                take(3)
                e.wait("params")
                e.wait("blk_ready")
                e.wait_bank_free("hid")
                for c in range(2):
                    for lp in range(L_CMP // 2):
                        ins = pe_.matmul(bank("hid")[:, c * 32:(c + 1) * 32], w1[:, c, lp, :],
                                         blk[:, c, lp, :, :], start=(lp == 0), stop=(lp == L_CMP // 2 - 1))
                fill(ins, "hid")
                for t in range(T):
                    use = f"pool_d{t}"
                    e.wait_bank_free(use)
                    for g in range(4):
                        dst = bank(use)[0:DK, g * P:(g + 1) * P]
                        chans = slice(g * DK, (g + 1) * DK)
                        ins = pe_.matmul(dst, zp[:, t, chans], pmx[:, t, g, :], start=True, stop=(t == 0))
                        if t:
                            ins = pe_.matmul(dst, zp[:, 0, chans], pmx[:, 2, g, :], start=False, stop=True)
                    fill(ins, use)
                take(3)
                e.wait_drained("hid")
                e.wait_bank_free("cmp_k")
                fill(pe_.matmul(bank("cmp_k")[0:32, 0:DK], hidT[:, 0, :, :], w2[:, 0, :],
                                start=True, stop=True), "cmp_k")
                e.wait("hidrep")
                e.wait_bank_free("cmp_v")
                fill(pe_.matmul(bank("cmp_v")[:, 0:DK], hid_rep, w2[:, 1, :], start=True, stop=True), "cmp_v")
                take(3)
                e.wait("sgw_ready")
                e.wait("vn_ready")
                e.wait_bank_free("mixed")
                for t in range(T):
                    for g in range(SGU_G):
                        at = t * SGU_W + g * 64
                        ins = pe_.matmul(bank("mixed")[:, at:at + 64], sgw[:, g, :], vn[:, t, g * 64:(g + 1) * 64],
                                         start=True, stop=True)
                fill(ins, "mixed")
                e.wait_drained("pool_d1")
                e.wait_bank_free("pool_y")
                for m in range(2):
                    for t in range(T):
                        for g in (2 * m, 2 * m + 1):
                            at = m * S + t * P
                            ins = pe_.matmul(bank("pool_y")[:, at:at + P], pw[0:DK, g, :], dT[0:DK, t, g, :],
                                             start=(g % 2 == 0), stop=(g % 2 == 1))
                fill(ins, "pool_y")
                take(2)
                e.wait("kcd_ready")
                e.wait_bank_free("kc_T")
                e.settle()
                transposes("kc_T", [kcd[0:32]], waited=True)
                take(2)
                e.wait_drained("q_T1")
                e.wait_drained("kc_T")
                e.wait_bank_free("cmp_s")
                for t in range(T):
                    for j in range(PAIRS):
                        at = t * P + j * 32
                        ins = pe_.matmul(bank("cmp_s")[:, at:at + 32], qT[:, j, t * P:(t + 1) * P], KcB[:, j // 2, :, :],
                                         start=True, stop=True)
                fill(ins, "cmp_s")

                def scores(u):
                    t, br, j = UNITS[u]
                    w = P * (t + 1)
                    e.wait_bank_free(f"s{u}")
                    fill(pe_.matmul(bank(f"s{u}")[:, 0:2 * w], qT[:, j, t * P:(t + 1) * P], kTm[:, br, j // 2, :, 0:w],
                                    start=True, stop=True), f"s{u}")

                e.wait_drained("kn_T1")
                scores(0)
                scores(1)
                for u, (t, br, j) in enumerate(UNITS):
                    take(2)
                    e.wait("p_exp", u + 1)
                    transposes(f"p_T{u}", [sring[:, u % 2, h, c * P:(c + 1) * P] for h in range(2) for c in range(t + 1)])
                    if u + 2 < len(UNITS):
                        scores(u + 2)
                    e.wait_drained(f"p_T{u}")
                    use = f"o{u // PAIRS}"
                    if j == 0:
                        e.wait_bank_free(use)
                    for h in range(2):
                        for c in range(t + 1):
                            at = (2 * j + h) * DK
                            g = j // 2
                            ins = pe_.matmul(bank(use)[:, at:at + DK], pT[:, u % 2, h * (t + 1) + c, :],
                                             zkv[:, c, 3 + 2 * br, g * DK:(g + 1) * DK], start=(c == 0), stop=(c == t))
                    if j == PAIRS - 1:
                        fill(ins, use)
                e.wait("pc_ready")
                transposes("pc_T", [sc[:, t, :, :] for t in range(T)])
                e.wait_drained("pc_T")
                e.wait_drained("cmp_v")
                for t in range(T):
                    e.wait_bank_free(f"oc{t}")
                    fill(pe_.matmul(bank(f"oc{t}"), pcT[:, t, :], vblk, start=True, stop=True), f"oc{t}")
                e.wait("o_ready")
                e.wait("ob_ready")
                rows_T(["br_T0", "br_T1"], ot)
                rows_T(["br_T2"], ob)
                rows_ready()
                take(16)
                e.wait("merged_ready")
                rows_T([f"mg_T{i}" for i in range(4)], merged)
                rows_ready()
                take(16)
                e.wait("xn_ready", 2)
                rows_T([f"xa_T{i}" for i in range(4)], xn)
                rows_ready()
                take(8)
                e.wait("xq_n")
                for i in range(2):
                    transposes(f"xq_T{i}", [xqt[:, t, h * XD:(h + 1) * XD] for h in (2 * i, 2 * i + 1) for t in range(T)])

                def xscores(u):
                    t, j = XUNITS[u]
                    e.wait_bank_free(f"xs{u}")
                    for h in range(2):
                        ins = pe_.matmul(bank(f"xs{u}")[:, h * MEM:(h + 1) * MEM], xqT[:, 2 * j + h, t * P:(t + 1) * P],
                                         mkT[:, 2 * j + h, :], start=True, stop=True)
                    fill(ins, f"xs{u}")

                e.wait_drained("xq_T1")
                e.wait_block("mem_v")
                xscores(0)
                xscores(1)
                for u, (t, j) in enumerate(XUNITS):
                    e.wait_drained(f"xs{u}")
                    transposes(f"xp_T{u}", [sring[:, u % 2, h, c * P:(c + 1) * P] for h in range(2) for c in range(2)])
                    if u + 2 < len(XUNITS):
                        xscores(u + 2)
                    e.wait_drained(f"xp_T{u}")
                    use = f"xo_{t}"
                    if j == 0:
                        e.wait_bank_free(use)
                    for h in range(2):
                        for c in range(2):
                            at = (2 * j + h) * XD
                            ins = pe_.matmul(bank(use)[:, at:at + XD], pT[:, u % 2, h * 2 + c, :],
                                             mv[:, c, at:at + XD], start=(c == 0), stop=(c == 1))
                    if j == 1:
                        fill(ins, use)
                e.wait("xo_ready")
                rows_T(["xo_T0", "xo_T1"], xo)
                rows_ready()
                take(8)
                e.wait("xn_ready", 3)
                rows_T([f"ff_T{i}" for i in range(4)], xn)
                rows_ready()
                take(16)
                e.wait_block("pq0")
                e.wait_block("pq1")
                rows_T([f"pq_T{i}" for i in range(4)], pq)
                for i in range(4):
                    e.wait_drained(f"pq_T{i}")
                for t in range(T):
                    for i in range(4):
                        use = f"ps{t}_{i}"
                        e.wait_bank_free(use)
                        for h in range(2):
                            ins = pe_.matmul(bank(use)[:, h * 256:(h + 1) * 256], pqT[:, 2 * i + h, t * P:(t + 1) * P],
                                             keys, start=True, stop=True)
                        fill(ins, use)
                def weights_step(i, s, half):
                    pe_.wait_ge(sig["g_out"].sem, layer * (2 * G_STEPS) + i * 4 + (half * G_STEPS + s + 1))
                    pe_.wait_ge(sig["hot_ready"].sem, layer * (4 * S) + i * (8 * G_TOK)
                                + (half * 2 * S + 2 * G_TOK * (s + 1)))
                    for r in range(G_TOK):
                        for c in range(PARTS):
                            at = KEYS + c * HALF
                            ins = pe_.matmul(aux[:, s % 2, r * HALF:(r + 1) * HALF], hots[:, s % 2, r, 0:KEYS],
                                             hots[:, s % 2, r, at:at + HALF], start=(c == 0), stop=(c == PARTS - 1))
                    ins.then_inc(sig["g_full"].sem, 1)

                for half in range(2):
                    if half:
                        e.wait("w_ready")
                        transposes("slot_T0", [ab[:, w, t, :, :] for w in range(2) for t in range(T)])
                        transposes("slot_T1", [cv[:, t, :, :] for t in range(T)])
                        for b in range(4):
                            pe_.wait_ge(drained[b].sem, drained[b].value(layer, drained[b].per))
                        e.settle()
                    with pe_.Fori(0, HALF // 4) as i:
                        for r in range(8):
                            q, kh = r // 2, r % 2
                            if kh == 0:
                                if half:
                                    weights_step(i, q, 0)
                                pe_.wait_ge(sig["u_out"].sem, layer * KEYS + i * 4 + (half * HALF + q + 1))
                            pe_.wait_ge(lo_ready, layer * PIECES + i * 8 + (HELD + PROJ + half * 2 * HALF + r + 1))
                            for k in range(4):
                                kt = kh * 4 + k
                                wh = w_hi[:, r % SLOTS, k * P:(k + 1) * P]
                                pe_.matmul(acc[:, q, 0:S], wh, h_hi[:, kt, :], start=(kt == 0), stop=False)
                                pe_.matmul(acc[:, q, 0:S], wh, h_lo[:, kt, :], start=False, stop=False)
                                ins = pe_.matmul(acc[:, q, 0:S], w_lo[:, r % SLOTS, k * P:(k + 1) * P], h_hi[:, kt, :],
                                                 start=False, stop=(kt == KD - 1))
                            ins.then_inc(used, 1)
                pe_.wait_ge(zero_set, 1)
                pe_.wait_ge(sig["u_out"].sem, layer * KEYS + (KEYS + 4))
                for q in range(4):
                    pe_.matmul(acc[:, q, :], zeros[:], zeros[:, 0:1].broadcast_to((P, COL)), start=True, stop=False)
                for half in range(2):
                    with pe_.Fori(0, HALF // 4) as i:
                        for r in range(8):
                            q, dh = r // 2, r % 2
                            if dh == 0:
                                if half == 0:
                                    weights_step(i, q, 1)
                                pe_.wait_ge(sig["eg_ready"].sem, layer * KEYS + i * 4 + (half * HALF + q + 1))
                            pe_.wait_ge(lo_ready, layer * PIECES + i * 8
                                        + (HELD + PROJ + U_PIECES + half * 2 * HALF + r + 1))
                            slot = r % SLOTS
                            for t in range(T):
                                ts = slice(t * P, (t + 1) * P)
                                dst = acc[:, 2 * t + dh, :]
                                pe_.matmul(dst, eg[:, q % 2, 0, ts], w_hi[:, slot, :], start=False, stop=False)
                                pe_.matmul(dst, eg[:, q % 2, 0, ts], w_lo[:, slot, :], start=False, stop=False)
                                ins = pe_.matmul(dst, eg[:, q % 2, 1, ts], w_hi[:, slot, :], start=False, stop=False)
                            ins.then_inc(used, 1)
                for q in range(4):
                    ins = pe_.matmul(acc[:, q, :], zeros[:], zeros[:, 0:1].broadcast_to((P, COL)), start=False, stop=True)
                ins.then_inc(sig["v_out"].sem, 1)

        @block.vector
        def _(dve):
            V = nc.vector
            V.memset(zeros[:], 0.0).then_inc(zero_set, 1)
            dve.wait_ge(const_in, 16)
            V.tensor_copy(iota_b[:], iota).then_inc(zero_set, 1)
            dve.wait_ge(zero_set, 2)
            dve.wait_ge(x_in, 16)
            for n, v in PRIMED.items():
                if n != "layer_free":
                    dve.sem_inc(sig[n].sem, v)
            for d in drained:
                dve.sem_inc(d.sem, 1)
            dve.sem_inc(sig["layer_free"].sem, 1)
            with dve.Fori(0, DEPTH) as layer:
                d = Engine(dve, layer, dve_step)
                hiT = [0]
                x_n = [0]

                def stt(o, i0, s, i1, op0, op1):
                    return V.scalar_tensor_tensor(out=o, in0=i0, scalar=s, in1=i1, op0=op0, op1=op1)

                def lo_T(name, k0, nk, gain=None, src=None, last=False):
                    hiT[0] += 1
                    d.wait("hi_T", hiT[0])
                    if src is None:
                        src = bank(name).rearrange("p (k t) -> p k t", t=S)
                    for k in range(nk):
                        dst, hi = h_lo[:, k0 + k, :], h_hi[:, k0 + k, :].bitcast(F32)
                        if gain is None:
                            ins = V.tensor_tensor(dst, src[:, k, :], hi, ALU.subtract)
                        else:
                            ins = stt(dst, src[:, k, :], col[:, gain + k:gain + k + 1], hi, ALU.mult, ALU.subtract)
                        if k == nk - 1 and name is not None:
                            d.step(ins, drains=name)
                        else:
                            d.step(ins)
                    if last:
                        sig["h_ready"].sent += 1
                        dve.sem_inc(sig["h_ready"].sem, 1)

                def mean(v, n, name):
                    d.step(V.tensor_scalar(v, v, 1.0 / n, EPS, ALU.mult, ALU.add), name)

                def rows_norm(v, src, dst, name):
                    for t in range(T):
                        d.step(V.tensor_scalar(dst[:, t, :], src[:, t, :], v[:, t:t + 1], None, ALU.mult),
                               name if t == T - 1 else None)

                def read_block(b, dsts):
                    d.wait_pieces(LAST[b])
                    n = len(dsts)
                    for i, (t, c0, c1, dst) in enumerate(dsts):
                        d.step(V.tensor_copy(dst, acc[:, PARITY[b] * 2 + t, c0:c1]), block=b if i == n - 1 else None)

                d.wait("x_sq", 1)
                mean(ssx, D, "x_mean")
                d.wait("x_sqrt", 1)
                d.step(V.reciprocal(ssx, ssx))
                rows_norm(ssx[:, 0:2], memx, memx, "mem_n")
                rows_norm(ssx[:, 2:4], X, xn, "xn_ready")
                for i in range(4):
                    lo_T(f"mem_T{i}", 2 * i, 2, C_MEM + 2 * i, last=i == 3)
                d.wait("params")
                zgf = zg_hi[:, :, :].bitcast(F32)
                d.step(V.tensor_copy(zg_hi[:, :, :], zgr))
                d.step(V.tensor_tensor(zg_lo[:, :, :], zgr, zgf, ALU.subtract), "zg_split")
                for br in range(2):
                    for h in range(2):
                        d.step(V.memset(kTm[(1 - h) * DK:(2 - h) * DK, br, :, h, :], 0.0))
                d.step(V.memset(hid_rep, 0.0))
                d.step(V.memset(hidT, 0.0))
                d.step(V.memset(KcB, 0.0))
                d.step(V.memset(blk, 0.0))
                d.step(V.tensor_tensor(sgw, sgw, trl.unsqueeze(1).broadcast_to((P, SGU_G, P)), ALU.mult), "sgw_ready")
                read_block("mem_k", [(t, 0, COL, mk[:, t, :]) for t in range(T)])
                read_block("mem_v", [(t, 0, COL, mv[:, t, :]) for t in range(T)])
                for i in range(4):
                    lo_T(f"mix_T{i}", 2 * i, 2, C_MIX + 2 * i, last=i == 3)
                mkh = mk.rearrange("p t (h c) -> p (t h) c", c=XD)
                tmph = tmp.rearrange("p t (h c) -> p (t h) c", c=XD)
                d.step(V.tensor_tensor(tmph, mkh, mkh, ALU.mult))
                d.step(V.tensor_reduce(ssh[:, 0:8], tmph, AX.X, ALU.add))
                mean(ssh[:, 0:8], XD, "mk_mean")
                d.wait("mk_sqrt")
                d.step(V.reciprocal(ssh[:, 0:8], ssh[:, 0:8]))
                d.step(V.tensor_tensor(mkh, mkh, ssh[:, 0:8].unsqueeze(2).broadcast_to((P, 8, XD)), ALU.mult), "mk_n")
                zkf = zkv.rearrange("p t c d -> p t (c d)")
                read_block("z_q", [(t, 0, COL, zq[:, t, :]) for t in range(T)])
                read_block("z_kv0", [(t, 0, COL, zkf[:, t, 0:COL]) for t in range(T)])
                for i in range(2):
                    d.wait_filled(f"mk_T{i}")
                    d.step(V.tensor_scalar(mkT[:, 2 * i:2 * i + 2, :], bank(f"mk_T{i}").rearrange("p (h m) -> p h m", h=2),
                                           col[:, C_XKN:C_XKN + 1], None, ALU.mult), drains=f"mk_T{i}")
                read_block("z_kv1", [(t, 0, 256, zkf[:, t, COL:768]) for t in range(T)]
                           + [(t, 256, COL, zp[:, t, :]) for t in range(T)])
                for t in range(T):
                    src = zkv[:, t, 0:2, :].rearrange("p c (g d) -> p (c g) d", g=2).unsqueeze(2).broadcast_to((P, 4, 2, DK))
                    d.step(V.tensor_copy(rawd[:, t], src), "rawd_ready" if t else None)
                zqh = zq.rearrange("p t (h c) -> p (t h) c", c=DK)
                tq = tmp.rearrange("p t (h c) -> p (t h) c", c=DK)
                d.step(V.tensor_tensor(tq, zqh, zqh, ALU.mult))
                d.step(V.tensor_reduce(ssh[:, 0:16], tq, AX.X, ALU.add))
                for br in range(2):
                    kk = zkv[:, :, 2 + 2 * br, :].rearrange("p t (g c) -> p t g c", g=2)
                    tk = tmp[:, 0, 0:256].rearrange("p (t g c) -> p t g c", t=2, g=2)
                    d.step(V.tensor_tensor(tk, kk, kk, ALU.mult))
                    d.step(V.tensor_reduce(ssh[:, 16 + 4 * br:20 + 4 * br].rearrange("p (t g) -> p t g", t=2), tk,
                                           AX.X, ALU.add))
                mean(ssh, DK, "qk_mean")
                d.wait("qk_sqrt")
                d.step(V.reciprocal(ssh, ssh))
                for t in range(T):
                    for br in range(2):
                        r = ssh[:, 16 + 4 * br + 2 * t:18 + 4 * br + 2 * t].unsqueeze(2).unsqueeze(3).broadcast_to((P, 2, 2, DK))
                        src = zkv[:, t, 2 + 2 * br, :].rearrange("p (g c) -> p g c", g=2).unsqueeze(2).broadcast_to((P, 2, 2, DK))
                        d.step(V.tensor_tensor(knd[:, t, br], src, r, ALU.mult), "knd_ready" if t and br else None)
                d.step(V.tensor_tensor(zqh, zqh, ssh[:, 0:16].unsqueeze(2).broadcast_to((P, 16, DK)), ALU.mult), "qn_ready")
                for i in range(2):
                    use = f"raw_T{i}"
                    d.wait_filled(use)
                    v = bank(use).rearrange("p (c s) -> p c s", c=2)
                    d.step(V.tensor_copy(KV2[0:DK, 2 * i:2 * i + 2, :], v[0:DK]))
                    d.step(V.tensor_copy(KV2[DK:P, 2 * i:2 * i + 2, 0:S - 1], v[DK:P, :, 1:S]), drains=use)
                k2 = KV2.rearrange("p c (n l r) -> p l c n r", l=8, r=2)
                for c in range(2):
                    for lh in range(2):
                        for g in range(KVG):
                            src = k2[:, :, 2 * c + g, lh:lh + N_CMP, 0]
                            add = pe[:, c, 8 * lh:8 * lh + 8].unsqueeze(2).broadcast_to((P, 8, N_CMP))
                            d.step(V.tensor_tensor(blk[:, c, 8 * lh:8 * lh + 8, g, 0:N_CMP], src, add, ALU.add),
                                   "blk_ready" if c and lh and g else None)
                for br in range(2):
                    use = f"kn_T{br}"
                    d.wait_filled(use)
                    v = bank(use).rearrange("p (g s) -> p g s", g=2)
                    for h in range(2):
                        ps = slice(h * DK, (h + 1) * DK)
                        ins = V.tensor_scalar(kTm[ps, br, :, h, :], v[ps], col[ps, C_KN + 1 + br:C_KN + 2 + br], None, ALU.mult)
                        if h:
                            d.step(ins, drains=use)
                        else:
                            d.step(ins)
                for i in range(2):
                    use = f"q_T{i}"
                    d.wait_filled(use)
                    d.step(V.tensor_scalar(qT[:, 2 * i:2 * i + 2, :], bank(use).rearrange("p (j s) -> p j s", j=2),
                                           col[:, C_QN:C_QN + 1], None, ALU.mult), drains=use)
                d.wait_block("z_sgu")
                for t in range(T):
                    d.step(V.bn_stats(bns[:, t, :], sg[:, t, SGU_W:2 * SGU_W]))
                    d.step(V.bn_aggr(mvr[:, t, :], bns[:, t, :]))
                d.step(V.tensor_scalar(mvr[:, :, 1], mvr[:, :, 1], 1.0, EPS, ALU.mult, ALU.add), "ln_mean")
                d.wait("ln_sqrt")
                d.step(V.reciprocal(mvr[:, :, 1], mvr[:, :, 1]))
                for t in range(T):
                    d.step(V.tensor_scalar(vn[:, t, :], sg[:, t, SGU_W:2 * SGU_W], mvr[:, t, 0:1], mvr[:, t, 1:2],
                                           ALU.subtract, ALU.mult))
                    d.step(V.tensor_tensor(vn[:, t, :], vn[:, t, :], lnr[:, 0:256], ALU.mult))
                    d.step(V.tensor_tensor(vn[:, t, :], vn[:, t, :], lnr[:, 256:512], ALU.add), "vn_ready" if t else None)
                d.wait_drained("hid")
                d.step(V.tensor_copy(hid_rep[:, :, :, 0:N_CMP],
                                     hidT[:, 1, :, 0:N_CMP].unsqueeze(2).broadcast_to((P, 2, 4, N_CMP))), "hidrep")
                for t in range(T):
                    use = f"pool_d{t}"
                    d.wait_filled(use)
                    d.step(V.tensor_copy(dT[0:DK, t], bank(use)[0:DK].rearrange("p (g s) -> p g s", g=4)), drains=use)
                d.wait_filled("cmp_k")
                d.step(V.tensor_copy(kcs[0:32], bank("cmp_k")[0:32, 0:DK]), drains="cmp_k")
                d.step(V.tensor_tensor(kcq[0:32], kcs[0:32], kcs[0:32], ALU.mult))
                d.step(V.tensor_reduce(ssk[0:32], kcq[0:32], AX.X, ALU.add))
                mean(ssk[0:32], DK, "kc_mean")
                d.wait_filled("cmp_v")
                d.step(V.tensor_tensor(vblk.rearrange("p (h c) -> p h c", h=8),
                                       bank("cmp_v")[:, 0:DK].unsqueeze(1).broadcast_to((P, 8, DK)),
                                       bmask.unsqueeze(2).broadcast_to((P, 8, DK)), ALU.mult), drains="cmp_v")
                d.wait("kc_sqrt")
                d.step(V.reciprocal(ssk[0:32], ssk[0:32]))
                d.step(V.tensor_scalar(kcd[0:32], kcs[0:32].unsqueeze(1).broadcast_to((32, 2, DK)), ssk[0:32], None, ALU.mult),
                       "kcd_ready")
                d.wait_filled("mixed")
                for t in range(T):
                    for g in range(SGU_G):
                        cs = slice(g * 64, (g + 1) * 64)
                        at = t * SGU_W + g * 64
                        ins = stt(ob[:, t, cs], bank("mixed")[:, at:at + 64], col[:, C_SB + g:C_SB + g + 1], sg[:, t, cs],
                                  ALU.add, ALU.mult)
                        if t == T - 1 and g == SGU_G - 1:
                            d.step(ins, drains="mixed")
                        else:
                            d.step(ins)
                sig["ob_ready"].sent += 1
                dve.sem_inc(sig["ob_ready"].sem, 1)
                d.wait_filled("pool_y")
                for m in range(2):
                    ins = V.tensor_scalar(yT[:, m, :], bank("pool_y")[:, m * S:(m + 1) * S],
                                          col[:, C_PSC + m:C_PSC + m + 1], None, ALU.mult)
                    if m:
                        d.step(ins, drains="pool_y")
                    else:
                        d.step(ins)
                d.wait_filled("kc_T")
                kct = bank("kc_T")[:, 0:32].rearrange("p (g n) -> p g n", g=2)
                for h in range(2):
                    ps = slice(h * DK, (h + 1) * DK)
                    ins = V.tensor_scalar(KcB[ps, :, h, 0:N_CMP], kct[ps, :, 0:N_CMP], col[ps, C_KN:C_KN + 1], None, ALU.mult)
                    if h:
                        d.step(ins, drains="kc_T")
                    else:
                        d.step(ins)
                d.wait_filled("cmp_s")
                for t in range(T):
                    ins = stt(sc[:, t], bank("cmp_s")[:, t * P:(t + 1) * P].rearrange("p (h n) -> p h n", h=8), DK ** -0.5,
                              cneg[:, t, :].unsqueeze(1).broadcast_to((P, 8, 16)), ALU.mult, ALU.add)
                    if t:
                        d.step(ins, drains="cmp_s")
                    else:
                        d.step(ins)
                scf = sc.rearrange("p t h n -> p (t h) n")
                cmb = cmx.unsqueeze(2).broadcast_to((P, 16, 16))
                d.step(V.tensor_reduce(cmx, scf, AX.X, ALU.max))
                d.step(V.tensor_tensor(scf, scf, cmb, ALU.subtract), "cs_ready")

                def unit_scores(u):
                    t, br, j = UNITS[u]
                    w = P * (t + 1)
                    use = f"s{u}"
                    mask = (cmask[:, P:2 * P] if t == 0 else cmask).unsqueeze(1).broadcast_to((P, 2, w))
                    d.wait_filled(use)
                    d.step(stt(sring[:, u % 2, :, 0:w], bank(use)[:, 0:2 * w].rearrange("p (h s) -> p h s", h=2), DK ** -0.5,
                               mask, ALU.mult, ALU.add), drains=use)
                    d.step(V.tensor_reduce(nmx[:, u % 2, :], sring[:, u % 2, :, 0:w], AX.X, ALU.max, negate=True), "s_ready")

                def combine(use, t, k, weights, first, done=None):
                    d.step(V.reciprocal(coef, weights))
                    d.step(V.tensor_tensor(coef, coef, ng[:, t, k:24:3], ALU.mult))
                    d.wait_filled(use)
                    dst = (ot if first else tmp)[:, t, :].rearrange("p (h c) -> p h c", h=8)
                    d.step(V.tensor_tensor(dst, bank(use).rearrange("p (h c) -> p h c", h=8),
                                           coef.unsqueeze(2).broadcast_to((P, 8, DK)), ALU.mult), drains=use)
                    if not first:
                        d.step(V.tensor_tensor(ot[:, t, :], ot[:, t, :], tmp[:, t, :], ALU.add), done)

                unit_scores(0)
                unit_scores(1)
                d.wait("cs_exp")
                d.step(V.tensor_tensor(sc, sc, cone.unsqueeze(2).broadcast_to((P, 2, 8, 16)), ALU.mult))
                d.step(V.tensor_reduce(cmx, scf, AX.X, ALU.add))
                d.step(V.tensor_scalar(cmx, cmx, 1e-30, None, ALU.max), "pc_ready")
                d.wait_drained("zg")
                for u, (t, br, j) in enumerate(UNITS):
                    use = f"p_T{u}"
                    d.wait_filled(use)
                    n = 2 * (t + 1)
                    d.step(V.tensor_copy(pT[:, u % 2, 0:n, :], bank(use)[:, 0:n * P].rearrange("p (n s) -> p n s", n=n)), drains=use)
                    if u + 2 < len(UNITS):
                        unit_scores(u + 2)
                    if j == PAIRS - 1:
                        combine(f"o{u // PAIRS}", t, 1 + br, sums[:, (t * 2 + br) % 2, :], br == 0)
                d.wait_filled("pc_T")
                d.step(V.tensor_copy(pcT, bank("pc_T")[:, 0:256].rearrange("p (t s) -> p t s", t=2)), drains="pc_T")
                for t in range(T):
                    combine(f"oc{t}", t, 0, cmx[:, t * 8:(t + 1) * 8], False, "o_ready" if t else None)
                for i in range(3):
                    lo_T(f"br_T{i}", 2 * i, 2)
                lo_T(None, 6, 2, src=yT, last=True)
                d.wait_block("z_m4")
                d.wait_block("z_m5")
                for n in range(2):
                    cs = slice(n * COL, (n + 1) * COL)
                    for i, b in enumerate((f"lift_a{n}", f"lift_b{n}", f"lift_c{n}")):
                        d.wait_pieces(LAST[b])
                        gs = slice(i * D + n * COL, i * D + (n + 1) * COL)
                        for t in range(T):
                            dst = merged[:, t, cs] if i == 0 else tmp[:, t, :]
                            d.step(V.tensor_tensor(dst, acc[:, PARITY[b] * 2 + t, :], gates[:, t, gs], ALU.mult),
                                   block=b if t else None)
                        if i:
                            d.step(V.tensor_tensor(merged[:, :, cs], merged[:, :, cs], tmp, ALU.add),
                                   "merged_ready" if i == 2 and n else None)
                for i in range(4):
                    lo_T(f"mg_T{i}", 2 * i, 2, last=i == 3)

                def add_block(b, n):
                    d.wait_pieces(LAST[b])
                    for t in range(T):
                        v = X[:, t, n * COL:(n + 1) * COL]
                        d.step(V.tensor_tensor(v, v, acc[:, PARITY[b] * 2 + t, :], ALU.add), block=b if t else None)

                def x_norm(k, tag, gain):
                    d.wait("x_sq", k)
                    mean(ssx[:, 2:4], D, "x_mean")
                    d.wait("x_sqrt", k)
                    d.step(V.reciprocal(ssx[:, 2:4], ssx[:, 2:4]))
                    rows_norm(ssx[:, 2:4], X, xn, "xn_ready")
                    for i in range(4):
                        lo_T(f"{tag}_T{i}", 2 * i, 2, gain + 2 * i, last=i == 3)

                add_block("out0", 0)
                add_block("out1", 1)
                x_norm(2, "xa", C_XA)
                read_block("xq", [(t, 0, COL, xqt[:, t, :]) for t in range(T)])
                xqh = xqt.rearrange("p t (h c) -> p (t h) c", c=XD)
                d.step(V.tensor_tensor(tmph, xqh, xqh, ALU.mult))
                d.step(V.tensor_reduce(ssh[:, 0:8], tmph, AX.X, ALU.add))
                mean(ssh[:, 0:8], XD, "xq_mean")
                d.wait("xq_sqrt")
                d.step(V.reciprocal(ssh[:, 0:8], ssh[:, 0:8]))
                d.step(V.tensor_tensor(xqh, xqh, ssh[:, 0:8].unsqueeze(2).broadcast_to((P, 8, XD)), ALU.mult), "xq_n")
                for i in range(2):
                    use = f"xq_T{i}"
                    d.wait_filled(use)
                    d.step(V.tensor_scalar(xqT[:, 2 * i:2 * i + 2, :], bank(use).rearrange("p (j s) -> p j s", j=2),
                                           col[:, C_XQN:C_XQN + 1], None, ALU.mult), drains=use)

                def x_scores(u):
                    d.wait_filled(f"xs{u}")
                    m = nmx[:, u % 2, :]
                    d.step(V.tensor_reduce(m, bank(f"xs{u}").rearrange("p (h m) -> p h m", h=2), AX.X, ALU.max, negate=True))
                    d.step(V.tensor_scalar(m, m, XD ** -0.5, None, ALU.mult), "xs_ready")

                x_scores(0)
                x_scores(1)
                for u, (t, j) in enumerate(XUNITS):
                    use = f"xp_T{u}"
                    d.wait_filled(use)
                    d.step(V.tensor_copy(pT[:, u % 2], bank(use).rearrange("p (n s) -> p n s", n=4)), drains=use)
                    if u + 2 < len(XUNITS):
                        x_scores(u + 2)
                    if j == 1:
                        d.wait_drained(f"xs{u}")
                        d.step(V.reciprocal(coef[:, 0:4], sums[:, t, 0:4]))
                        d.wait_filled(f"xo_{t}")
                        d.step(V.tensor_tensor(xo[:, t, :].rearrange("p (h c) -> p h c", h=4),
                                               bank(f"xo_{t}").rearrange("p (h c) -> p h c", h=4),
                                               coef[:, 0:4].unsqueeze(2).broadcast_to((P, 4, XD)), ALU.mult),
                               drains=f"xo_{t}")
                sig["xo_ready"].sent += 1
                dve.sem_inc(sig["xo_ready"].sem, 1)
                for i in range(2):
                    lo_T(f"xo_T{i}", 2 * i, 2, last=i == 1)
                add_block("xo0", 0)
                add_block("xo1", 1)
                x_norm(3, "ff", C_FFN)
                for n in range(2):
                    read_block(f"pq{n}", [(t, 0, COL, pq[:, t, n * COL:(n + 1) * COL]) for t in range(T)])
                for i in range(4):
                    use = f"pq_T{i}"
                    d.wait_filled(use)
                    d.step(V.tensor_copy(pqT[:, 2 * i:2 * i + 2, :], bank(use).rearrange("p (j s) -> p j s", j=2)), drains=use)
                for t in range(T):
                    for i in range(4):
                        use = f"ps{t}_{i}"
                        d.wait_filled(use)
                        d.step(V.tensor_copy(rs[:, 2 * i:2 * i + 2], bank(use).rearrange("p (h f k) -> p h f k", h=2, f=2)),
                               drains=use)
                    for h in range(PH):
                        for f in range(2):
                            v = rs[:, h, f, :]
                            d.settle()
                            d.step(V.max(tv[:, h, f, 0:8], v))
                            d.step(V.max_index(ti[:, h, f, 0:8], tv[:, h, f, 0:8], v))
                            d.step(V.match_replace(v, tv[:, h, f, 0:8], v, LOWEST))
                            d.step(V.max(tv[:, h, f, 8:16], v))
                            d.step(V.max_index(ti[:, h, f, 8:16], tv[:, h, f, 8:16], v))
                    d.step(V.tensor_copy(topf[:], topi[:]))
                    for h in range(PH):
                        d.step(V.tensor_tensor(cand[:, h], tv[:, h, 0, :].unsqueeze(2).broadcast_to((P, 16, 16)),
                                               tv[:, h, 1, :].unsqueeze(1).broadcast_to((P, 16, 16)), ALU.add))
                    for h in range(PH):
                        v = cand[:, h].rearrange("p i j -> p (i j)")
                        c = ci[:, h * 16:(h + 1) * 16]
                        w = cv[:, t, h, :]
                        d.step(V.max(w[:, 0:8], v))
                        d.step(V.max_index(c[:, 0:8], w[:, 0:8], v))
                        d.step(V.match_replace(v, w[:, 0:8], v, LOWEST))
                        d.step(V.max(w[:, 8:16], v))
                        d.step(V.max_index(c[:, 8:16], w[:, 8:16], v))
                    d.step(V.tensor_scalar(cia, ci, 4, None, ALU.logical_shift_right))
                    d.step(V.tensor_copy(iab[:, 0, :], cia))
                    d.step(V.tensor_scalar(cia, ci, 15, None, ALU.bitwise_and))
                    d.step(V.tensor_copy(iab[:, 1, :], cia))
                    for f in range(2):
                        d.step(V.tensor_tensor(onehot, iab[:, f, :].unsqueeze(2).broadcast_to((P, 128, 16)),
                                               iota16.unsqueeze(1).broadcast_to((P, 128, 16)), ALU.is_equal))
                        oh = onehot.rearrange("p (h k) j -> p h k j", h=PH)
                        d.step(V.tensor_tensor(oh, oh, tf[:, :, f, :].unsqueeze(2).broadcast_to((P, PH, 16, 16)), ALU.mult))
                        d.step(V.tensor_reduce(ab[:, f, t].rearrange("p h k -> p (h k)"), onehot, AX.X, ALU.add))
                cvf = cv[:, :, :, :].rearrange("p t h k -> p (t h) k")
                d.step(V.tensor_reduce(cmx, cvf, AX.X, ALU.max))
                d.step(V.tensor_tensor(cvf, cvf, cmb, ALU.subtract), "cv_ready")
                d.wait("w_exp")
                d.step(V.tensor_reduce(cmx, cvf, AX.X, ALU.add))
                d.step(V.reciprocal(cmx, cmx))
                d.step(V.tensor_tensor(cvf, cvf, cmb, ALU.mult), "w_ready")
                d.wait_filled("slot_T0")
                d.step(V.tensor_copy(slot_a[:], bank("slot_T0")[:, 0:S]))
                d.step(V.tensor_copy(slot_b[:], bank("slot_T0")[:, S:2 * S]), drains="slot_T0")
                d.wait_filled("slot_T1")
                d.step(V.tensor_copy(slot_w, bank("slot_T1")[:, 0:S]), drains="slot_T1")
                for c in range(PARTS):
                    d.step(V.tensor_copy(slot_parts[:, c, :], slot_w))
                    if c < PARTS - 1:
                        d.step(V.tensor_tensor(slot_w, slot_w, slot_parts[:, c, :], ALU.subtract))

                def one_hots(i, s, half):
                    for r in range(G_TOK):
                        t = i * (4 * G_TOK) + (s * G_TOK + r)
                        one = lambda v: v[:, bass.ds(t, 1)]
                        V.tensor_scalar(hots[:, s % 2, r, 0:KEYS], iota_b[:], one(slot_b), None,
                                        ALU.is_equal).then_inc(sig["hot_ready"].sem, 1)
                        stt(hots[:, s % 2, r, KEYS:HOT].rearrange("p (c a) -> p c a", c=PARTS),
                            iota_b[:, half * HALF:(half + 1) * HALF].unsqueeze(1).broadcast_to((P, PARTS, HALF)), one(slot_a),
                            slot_parts[:, :, bass.ds(t, 1)].broadcast_to((P, PARTS, HALF)),
                            ALU.is_equal, ALU.mult).then_inc(sig["hot_ready"].sem, 1)

                def weigh(i, s, half):
                    dve.wait_ge(sig["g_full"].sem, layer * (2 * G_STEPS) + i * 4 + (half * G_STEPS + s + 1))
                    v = experts[:, half * HALF:(half + 1) * HALF, bass.ds(i * (4 * G_TOK) + s * G_TOK, G_TOK)]
                    v = v.rearrange("p a t -> p t a")
                    V.tensor_tensor(v, v, aux[:, s % 2, 0:G_TOK * HALF].rearrange("p (t a) -> p t a", t=G_TOK),
                                    ALU.mult).then_inc(sig["g_out"].sem, 1)

                def weighted(i, q):
                    src = experts[:, bass.ds(i * 4 + q, 1), :].rearrange("p o t -> p (o t)")
                    dve.wait_ge(sig["eg_hi"].sem, layer * KEYS + i * 4 + (q + 1))
                    V.tensor_tensor(eg[:, q % 2, 1, :], src, eg[:, q % 2, 0, :].bitcast(F32),
                                    ALU.subtract).then_inc(sig["eg_ready"].sem, 1)

                d.wait("u_out", HALF)
                one_hots(0, 0, 0)
                one_hots(0, 1, 0)
                with dve.Fori(0, G_STEPS // 4 - 1) as i:
                    for q in range(4):
                        weigh(i, q, 0)
                        one_hots(i, q + 2, 0)
                last = G_STEPS // 4 - 1
                for q in range(4):
                    weigh(last, q, 0)
                    if q < 2:
                        one_hots(last, q + 2, 0)
                d.wait("u_out", KEYS)
                d.wait("g_out", G_STEPS)
                one_hots(0, 0, 1)
                weighted(0, 0)
                one_hots(0, 1, 1)
                with dve.Fori(0, G_STEPS // 4 - 1) as i:
                    for q in range(4):
                        weigh(i, q, 1)
                        weighted(i, q + 1)
                        one_hots(i, q + 2, 1)
                for q in range(4):
                    weigh(last, q, 1)
                    if q < 3:
                        weighted(last, q + 1)
                    if q < 2:
                        one_hots(last, q + 2, 1)
                sig["hot_ready"].sent += 4 * S
                sig["g_out"].sent += 2 * G_STEPS
                d.wait("g_out")
                d.settle()
                with dve.Fori(HALF // 4, KEYS // 4) as i:
                    for q in range(4):
                        weighted(i, q)
                d.wait("eg_ready")
                d.wait("v_out")
                for t in range(T):
                    d.step(V.tensor_tensor(X[:, t, :].rearrange("p (n c) -> p n c", n=2),
                                           X[:, t, :].rearrange("p (n c) -> p n c", n=2),
                                           acc[:, 2 * t:2 * t + 2, :], ALU.add), "layer_free" if t else None)
                d.settle()
                dve.sem_clear(dve_step)
        for n in ("x_sq", "hi_T", "s_ready", "xs_ready", "h_ready", "p_exp", "acc_free0", "acc_free1", "g_out", "xn_ready"):
            assert sig[n].sent == sig[n].per, (n, sig[n].sent, sig[n].per)
        for s in filled + drained:
            assert s.sent == s.per, ([f.sent for f in filled], [f.sent for f in drained], n_uses)


def constants():
    c = np.zeros((P, K_END), np.float32)
    r = np.arange(P)
    c[:, K_ID:K_ID + P] = np.eye(P)
    c[:, K_IO:K_IO + P] = r[None, :]
    c[:, K_CM + P:K_CM + 2 * P] = np.where(r[None, :] <= r[:, None], 0.0, NEG)
    end = np.arange(NP_) * D_CMP + L_CMP - 1
    for t in range(T):
        ok = (end[None, :] <= (t * P + r)[:, None]) & (np.arange(NP_) < N_CMP)[None, :]
        c[:, K_CN + t * NP_:K_CN + (t + 1) * NP_] = np.where(ok, 0.0, NEG)
        c[:, K_C1 + t * NP_:K_C1 + (t + 1) * NP_] = ok
    c[:, K_BM:K_BM + HEADS] = (r[:, None] // NP_) == np.arange(HEADS)[None, :]
    c[:, K_I16:K_I16 + TOPK] = np.arange(TOPK)[None, :]
    tril = (r[:, None] <= r[None, :]).astype(np.float32)
    pm = np.zeros((3, len(WINDOWS), S // T, P), np.float32)
    for g, w in enumerate(WINDOWS):
        m = np.zeros((S, S), np.float32)
        for t in range(S):
            m[max(0, t - w + 1):t + 1, t] = np.float32(1.0) / min(t + 1, w)
            m[t, t] -= 1.0
        pm[0, g], pm[1, g], pm[2, g] = m[:P, :P], m[P:, P:], m[:P, P:]
    return c, tril, np.ascontiguousarray(pm.transpose(2, 0, 1, 3)).reshape(P, -1)


def layouts(inp):
    def proj(w, n):
        return w[:, n * COL:(n + 1) * COL].reshape(-1, P, COL)

    stream = np.empty((DEPTH, PIECES, P, COL), np.float32)
    for l in range(DEPTH):
        w_in = inp["w_in"][l]
        q0, kv0, g0 = 0, 512, 512 + 768
        sg0 = g0 + 24
        p0, m0 = sg0 + 512, sg0 + 512 + 256
        z = [w_in[:, q0:kv0], w_in[:, kv0:kv0 + 512], np.concatenate([w_in[:, kv0 + 512:g0], w_in[:, p0:m0]], 1),
             w_in[:, sg0:p0]] + [w_in[:, m0 + i * 512:m0 + (i + 1) * 512] for i in range(6)]
        parts = [proj(inp["xa_wk"][l], 0), proj(inp["xa_wv"][l], 0)] + [proj(w, 0) for w in z]
        for n in range(2):
            parts += [proj(inp[k][l], n) for k in ("lift_a", "lift_b", "lift_c")]
        parts += [proj(inp["w_out"][l], n) for n in range(2)] + [proj(inp["xa_wq"][l], 0)]
        parts += [proj(inp["xa_wo"][l], n) for n in range(2)] + [proj(inp["peer_wq"][l], n) for n in range(2)]
        stream[l, :PROJ] = np.concatenate(parts)
        u = inp["peer_u"][l].reshape(KEYS, KEYS, 2, 4, P).transpose(0, 2, 4, 3, 1)
        stream[l, PROJ:PROJ + U_PIECES] = u.reshape(U_PIECES, P, COL)
        v = inp["peer_v"][l].reshape(KEYS, KEYS, 2, COL).transpose(0, 2, 1, 3)
        stream[l, PROJ + U_PIECES:] = v.reshape(V_PIECES, P, COL)
    stream = stream.reshape(DEPTH * CHUNKS, PER_CHUNK, P, COL).transpose(0, 2, 1, 3).reshape(DEPTH * CHUNKS, P, -1)

    cols = np.zeros((DEPTH, P, C_END), np.float32)
    for name, c in (("mix_norm", C_MIX), ("xa_norm", C_XA), ("ffn_norm", C_FFN), ("mem_norm", C_MEM)):
        cols[:, :, c:c + KD] = inp[name].reshape(DEPTH, KD, P).transpose(0, 2, 1)
    cols[:, :, C_QN] = np.tile(inp["nsa_q_norm"], (1, 2))
    cols[:, :, C_KN:C_KN + 3] = np.tile(inp["nsa_k_norm"], (1, 1, 2)).transpose(0, 2, 1)
    cols[:, :, C_XQN], cols[:, :, C_XKN] = inp["xa_q_norm"], inp["xa_k_norm"]
    cols[:, :, C_PSC:C_PSC + 2] = inp["pool_scale"].reshape(DEPTH, 2, P).transpose(0, 2, 1)
    cols[:, :, C_SB:C_SB + 4] = inp["sgu_b"].transpose(0, 2, 1)

    w1 = inp["cmp_w1"].reshape(DEPTH, 2, 16, 2, DK, CMP_HID).transpose(0, 3, 4, 1, 2, 5).reshape(DEPTH, P, -1)
    w2 = inp["cmp_w2"].transpose(0, 2, 1, 3).reshape(DEPTH, P, -1)
    pe = inp["cmp_pe"].reshape(DEPTH, 2, 16, 2, DK).transpose(0, 3, 4, 1, 2).reshape(DEPTH, P, -1)
    parb = np.concatenate([w1, w2, pe], 2)
    sgw = inp["sgu_w"].transpose(0, 3, 1, 2).reshape(DEPTH, P, -1)
    pw = np.zeros((DEPTH, P, 4, 2, DK), np.float32)
    for g in range(4):
        pw[:, :DK, g, g % 2, :] = inp["pool_w"][:, g]
    keys = np.zeros((DEPTH, 2, DK, 2, KEYS), np.float32)
    keys[:, 0, :, 0], keys[:, 1, :, 1] = (inp[k].transpose(0, 2, 1) for k in ("peer_keys1", "peer_keys2"))
    parr = np.concatenate([sgw, pw.reshape(DEPTH, P, -1), keys.reshape(DEPTH, P, -1)], 2)
    lnrow = np.concatenate([inp["sgu_ln_g"], inp["sgu_ln_b"]], 1)
    zgw = inp["w_in"][:, :, 1280:1304].reshape(DEPTH, KD, P, 24).transpose(0, 2, 1, 3).reshape(DEPTH, P, -1)
    consts, tril, pm = constants()
    arrays = dict(x=inp["x"][0], mem=inp["mem"][0], stream=stream, cols=cols, parb=parb, parr=parr, lnrow=lnrow,
                  zgw=zgw, consts=consts, pm=pm, tril=tril)
    return {k: np.ascontiguousarray(v) for k, v in arrays.items()}


_INS = ["x", "mem", "stream", "cols", "parb", "parr", "lnrow", "zgw", "consts", "pm", "tril"]


def kernel(**inputs):
    import concourse.bacc as _bacc
    from concourse.bass_utils import run_bass_kernel_spmd as _run

    arrays = layouts({k: np.asarray(v) for k, v in inputs.items()})
    nc = _bacc.Bacc("TRN2", target_bir_lowering=False, num_devices=1)
    aps = {k: nc.dram_tensor(k + "_dram", arrays[k].shape, mybir.dt.float32, kind="ExternalInput").ap() for k in _INS}
    out = nc.dram_tensor("out_dram", (S, D), mybir.dt.float32, kind="ExternalOutput").ap()
    trunk(nc, out=out, **aps)
    r = _run(nc, [{k + "_dram": arrays[k] for k in _INS}], core_ids=[0])
    return r.results[0]["out_dram"].reshape(1, S, D)
```

```python
from contextlib import ExitStack

import numpy as np
import concourse.bass as bass
from concourse import mybir

F32 = mybir.dt.float32
F32R = mybir.dt.float32r
BF16 = mybir.dt.bfloat16
U32 = mybir.dt.uint32
ALU = mybir.AluOpType
ACT = mybir.ActivationFunctionType
AX = mybir.AxisListType

P = 128
DEPTH, D, S, MEM = 2, 1024, 256, 256
EPS, NEG = 1e-6, -1e30
HEADS, DK, KVG = 8, 64, 2
PAIRS = HEADS // 2
L_CMP, D_CMP, CMP_HID = 32, 16, 128
N_CMP = (S - L_CMP) // D_CMP + 1
NP_ = 16
SGU_W, SGU_G, POOL_W = 256, 4, 256
WINDOWS = (2, 4, 8, 16)
XH, XD = 4, 128
PH, KEYS, TOPK = 8, 128, 16
T = S // P
KD = D // P
COL = 512
LOWEST = -3.0e38

PER_CHUNK = 2
SLOTS = 4
RAW = 4
HELD = RAW * PER_CHUNK
BLOCKS = (["mem_k", "mem_v", "z_q", "z_kv0", "z_kv1", "z_sgu"] + [f"z_m{i}" for i in range(6)]
          + ["lift_b0", "lift_c0", "lift_a0", "lift_b1", "lift_c1", "lift_a1"]
          + ["out0", "out1", "xq", "xo0", "xo1", "pq0", "pq1"])
DEPTH_OF = {"lift_a": 4, "lift_b": 2, "lift_c": 2, "xo": 4}
ROWS = dict(mem_k=("mem", 0), mem_v=("mem", 0), lift_a=("br", 0), lift_b=("br", 4), lift_c=("br", 6), out=("mg", 0),
            xq=("xa", 0), xo=("xo", 0), pq=("fu", 0))
SECOND = ("mg", "fu")


def pieces_of(block):
    return DEPTH_OF.get(block.rstrip("01"), KD)


FIRST = {}
_n = 0
for _b in BLOCKS:
    FIRST[_b] = _n
    _n += pieces_of(_b)
PROJ = _n
U_PIECES = V_PIECES = KEYS * 2
PIECES = PROJ + U_PIECES + V_PIECES
CHUNKS = PIECES // PER_CHUNK
LAST = {b: FIRST[b] + pieces_of(b) for b in BLOCKS}
SHARED = PROJ + U_PIECES + V_PIECES // 2
PARITY = {b: i % 2 for i, b in enumerate(BLOCKS)}
assert PROJ % HELD == 0

USES = [(f"mem_T{i}", i) for i in range(4)] + [(f"mix_T{i}", i) for i in range(4)]
USES += [("mk_T0", 0), ("mk_T1", 1), ("zg", 2), ("raw_T0", 0), ("raw_T1", 1), ("kn_T0", 2), ("kn_T1", 3),
         ("q_T0", 0), ("q_T1", 1), ("hid", 2), ("pool_d0", 0), ("pool_d1", 1), ("cmp_k", 2), ("cmp_v", 3),
         ("mixed", 0), ("pool_y", 1), ("kc_T", 2), ("cmp_s", 3)]
UNITS = [(t, br, j) for t in range(T) for br in range(2) for j in range(PAIRS)]
USES += [("s0", 0), ("s1", 1)]
for _u in range(len(UNITS)):
    USES += [(f"p_T{_u}", 2)]
    if _u + 2 < len(UNITS):
        USES += [(f"s{_u + 2}", _u % 2)]
    if _u % PAIRS == 0:
        USES += [(f"o{_u // PAIRS}", 3)]
    USES += {1: [("pc_T", 2)], 2: [("oc0", 2)], 3: [("oc1", 2)]}.get(_u, [])
USES += [("br_T2", 0), ("br_T0", 1), ("br_T1", 2)]
USES += [(f"mg_T{i}", (i + 3) % 4) for i in range(4)] + [(f"xa_T{i}", (i + 3) % 4) for i in range(4)]
USES += [("xq_T0", 0), ("xq_T1", 1)]
XUNITS = [(t, j) for t in range(T) for j in range(XH // 2)]
USES += [("xs0", 0), ("xs1", 1)]
for _u in range(len(XUNITS)):
    USES += [(f"xp_T{_u}", 2)]
    if _u + 2 < len(XUNITS):
        USES += [(f"xs{_u + 2}", _u % 2)]
    if _u % 2 == 0:
        USES += [(f"xo_{_u // 2}", 3)]
USES += [("xo_T0", 0), ("xo_T1", 1)]
USES += [(f"{r}_T{i}", (i + 2) % 4) for r in ("fu", "ff") for i in range(4)]
USES += [(f"pq_T{i}", i) for i in range(4)]
USES += [(f"ps0_{i}", i) for i in range(4)] + [(f"ps1_{i}", i) for i in range(4)]
USES += [("slot_T0", 0), ("slot_T1", 1)]
G_TOK = 4
G_STEPS = S // G_TOK
HALF = KEYS // 2
LOAD_AT, NORM_AT, MEM_AT = HALF + 4, HALF + 12, (HALF + 20, HALF + 28, HALF + 36, HALF + 44)
PARTS = 3
EXP_AT, SLOTS_AT = 52, 56
HOT = KEYS + PARTS * HALF
assert G_STEPS == HALF

C_MIX, C_XA, C_FFN, C_MEM = 0, 8, 16, 24
C_QN, C_KN, C_XQN, C_XKN, C_PSC, C_SB, C_END = 32, 33, 36, 37, 38, 40, 44
K_ID, K_IO, K_CM, K_CN, K_C1, K_BM, K_I16 = 0, 128, 256, 512, 544, 576, 584
K_END = K_I16 + 16 + 1

OWN = [("memx", T * D), ("xn", T * D), ("mk", T * 512), ("mv", T * 512), ("mkT", XH * MEM), ("zkv", T * 768),
       ("zp", T * POOL_W), ("gates", T * 3072), ("ng", T * 24), ("knd", T * 512), ("KV2", 4 * S), ("blk", 2 * 16 * 32),
       ("w1", 4096), ("w2", 128), ("pe", 32), ("kTm", 2 * 4 * S), ("qT", PAIRS * S), ("ob", T * SGU_W),
       ("vn", T * SGU_W), ("sgw", 512), ("pw", 512), ("keys", 256), ("lnrow", 512), ("zgw", 192), ("tril", 128),
       ("pm", 1536), ("tmp", T * 512), ("cmp", 1024)]
REUSE = {"zq": ("memx", 0), "sg": ("memx", 1024), "rawd": ("mk", 0), "dT": ("mk", 0), "o": ("knd", 0),
         "junk": ("kTm", 0), "merged": ("w1", 0), "xo": ("gates", 4096), "pq": ("gates", 0), "pqT": ("gates", 2048),
         "sring": ("KV2", 0), "pT": ("blk", 0), "yT": ("vn", 0), "vblk": ("lnrow", 0),
         "rout": ("merged", 0), "topi": ("w1", 2048)}
OFF = {}
_o = 0
for _name, _size in OWN:
    OFF[_name] = _o
    _o += _size
for _name, (_first, _in) in REUSE.items():
    OFF[_name] = OFF[_first] + _in
assert min(OFF["rout"], OFF["topi"]) >= KEYS * S // 2
BIG = KEYS * S
assert _o <= BIG, _o


class Signal:

    def __init__(self, sem, per, primed=0):
        self.sem, self.per, self.primed, self.sent = sem, per, primed, 0

    def value(self, layer, k):
        return layer * self.per + (k + self.primed)


def trunk(nc, x, mem, stream, cols, parb, parr, lnrow, zgw, consts, pm, tril, out):
    ctx = ExitStack()
    with ctx:
        def sb(name, shape, dt=F32):
            return ctx.enter_context(nc.sbuf_tensor(name, shape, dt))

        def sem(name):
            return ctx.enter_context(nc.semaphore(name))

        raw = sb("raw", [P, RAW, PER_CHUNK, COL])
        w_hi = sb("w_hi", [P, SLOTS, COL], F32R)
        w_lo = sb("w_lo", [P, SLOTS, COL], F32R)
        X = sb("X", [P, T, D])
        h_hi = sb("h_hi", [P, KD, S], F32R)
        h_lo = sb("h_lo", [P, KD, S], F32R)
        big = sb("big", [P, BIG])
        eg = sb("eg", [P, 2, 2, S], F32R)
        cst = sb("cst", [P, K_END])
        col = sb("col", [P, C_END])
        zg_hi = sb("zg_hi", [P, KD, 24], F32R)
        zg_lo = sb("zg_lo", [P, KD, 24], F32R)
        zeros = sb("zeros", [P, 128], BF16)
        iota_b = sb("iota_b", [P, P], BF16)
        hots = sb("hots", [P, 2, G_TOK, HOT], BF16)
        h2_lo = sb("h2_lo", [P, KD // 2, S], F32R)
        topv = sb("topv", [P, PH * 2 * 16])
        topf = sb("topf", [P, PH * 2 * 16])
        cv = sb("cv", [P, T, PH, TOPK])
        ab = sb("ab", [P, 2, T, PH, TOPK])
        st = sb("st", [P, 96])
        tblw = cst[:, K_END - 1:K_END]

        def region(name, size, *dims):
            v = big[:, OFF[name]:OFF[name] + size]
            if not dims:
                return v
            names = "abcde"[:len(dims)]
            return v.rearrange(f"p ({' '.join(names)}) -> p {' '.join(names)}", **dict(zip(names[1:], dims[1:])))

        memx, xn, junk = (region(n, T * D, T, D) for n in ("memx", "xn", "junk"))
        mk, mv, zq, sg, ot, xo, tmp = (region(n, T * 512, T, 512) for n in ("mk", "mv", "zq", "sg", "o", "xo", "tmp"))
        mkT = region("mkT", XH * MEM, XH, MEM)
        zkv = region("zkv", T * 768, T, 6, 128)
        zp = region("zp", T * POOL_W, T, POOL_W)
        gates = region("gates", T * 3072, T, 3072)
        ng = region("ng", T * 24, T, 24)
        rawd = region("rawd", T * 512, T, 4, 2, DK)
        knd = region("knd", T * 512, T, 2, KVG, 2, DK)
        KV2 = region("KV2", 4 * S, 4, S)
        blk = region("blk", 1024, 2, 16, 2, 16)
        w1 = region("w1", 4096, 2, 16, 128)
        w2 = region("w2", 128, 2, DK)
        pe = region("pe", 32, 2, 16)
        kTm = region("kTm", 2 * 4 * S, 2, KVG, 2, S)
        qT = region("qT", PAIRS * S, PAIRS, S)
        sring = region("sring", 1024, 2, 2, 256)
        pT = region("pT", 1024, 2, 4, 128)
        vblk = region("vblk", 512)
        ob, vn = (region(n, T * SGU_W, T, SGU_W) for n in ("ob", "vn"))
        dT = region("dT", T * 512, T, 4, P)
        yT = region("yT", 512, 2, S)
        sgw = region("sgw", 512, SGU_G, P)
        pw = region("pw", 512, 4, P)
        keys = region("keys", 256)
        lnr = region("lnrow", 512)
        zgr = region("zgw", 192, KD, 24)
        trl = region("tril", 128)
        pmx = region("pm", 1536, 3, 4, P)
        merged = region("merged", T * D, T, D)
        pq = region("pq", T * D, T, D)
        pqT = region("pqT", PH * S, PH, S)
        cm = big[:, OFF["cmp"]:OFF["cmp"] + 1024]
        hidT = cm[:, 0:64].rearrange("p (c g n) -> p c g n", c=2, g=2)
        hid_rep = cm[:, 64:192].rearrange("p (g r n) -> p g r n", g=2, r=4)
        kcs = cm[:, 192:256]
        kcq = cm[:, 256:320]
        kcd = cm[:, 320:448].rearrange("p (a d) -> p a d", a=2)
        KcB = cm[:, 448:512].rearrange("p (g h n) -> p g h n", g=2, h=2)
        sc = cm[:, 512:768].rearrange("p (t h n) -> p t h n", t=2, h=8)
        pcT = cm[:, 768:1024].rearrange("p (t s) -> p t s", t=2)
        h2_hi = eg[:, :, :, :].rearrange("p a b s -> p (a b) s")
        rout = region("rout", 2048)
        topi = region("topi", PH * 2 * 16).bitcast(U32)

        def rows_of(tag, kt):
            return (h2_hi, h2_lo) if tag in SECOND and kt < KD // 2 else (h_hi, h_lo)

        xqt, xqT = zq, region("qT", XH * S, XH, S)
        experts = big[:, :].rearrange("p (a t) -> p a t", t=S)

        ident = cst[:, K_ID:K_ID + P]
        iota = cst[:, K_IO:K_IO + P]
        cmask = cst[:, K_CM:K_CM + 256]
        cneg = cst[:, K_CN:K_CN + 32].rearrange("p (t n) -> p t n", t=2)
        cone = cst[:, K_C1:K_C1 + 32].rearrange("p (t n) -> p t n", t=2)
        bmask = cst[:, K_BM:K_BM + 8]
        iota16 = cst[:, K_I16:K_I16 + 16]

        rs = rout[:, :].rearrange("p (h f k) -> p h f k", h=PH, f=2)
        cand = rout[:, :].rearrange("p (h i j) -> p h i j", h=PH, i=TOPK)
        onehot = rout[:, :].rearrange("p (m j) -> p m j", j=TOPK)
        slot_a, slot_b = topv, topf
        slot_w = cv[:, :, :, :].rearrange("p t h k -> p (t h k)")
        slot_parts = ab[:, :, :, :, :].rearrange("p w t h k -> p (w t h k)").bitcast(BF16)[:, 0:PARTS * S].rearrange(
            "p (c t) -> p c t", c=PARTS)
        tv = topv[:, :].rearrange("p (h f k) -> p h f k", h=PH, f=2)
        ti = topi[:, :].rearrange("p (h f k) -> p h f k", h=PH, f=2)
        tf = topf[:, :].rearrange("p (h f k) -> p h f k", h=PH, f=2)
        iab = topv[:, :].rearrange("p (w m) -> p w m", w=2)
        ci = topi[:, 0:128]
        cia = topi[:, 128:256]

        ssm = st[:, 0:2]
        ssx = st[:, 2:4]
        ssh = st[:, 4:28]
        coef = st[:, 28:36]
        nmx = st[:, 36:40].rearrange("p (r h) -> p r h", r=2)
        bns = st[:, 40:52].rearrange("p (t s) -> p t s", t=2)
        mvr = st[:, 52:56].rearrange("p (t s) -> p t s", t=2)
        xsq = st[:, 90:94]
        ssk = st[:, 56:57]
        cmx = st[:, 58:74]
        sums = st[:, 74:90].rearrange("p (r h) -> p r h", r=2)

        acc = ctx.enter_context(nc.psum_tensor("acc", [P, 4, COL], F32))
        aux = ctx.enter_context(nc.psum_tensor("aux", [P, 4, COL], F32))

        chunk_in = [sem(f"chunk_in{r}") for r in range(RAW)]
        hi_ready = sem("hi_ready")
        lo_ready = sem("lo_ready")
        lo_shared = sem("lo_shared")
        used = sem("used")

        PER = dict(
            layer_free=2,
            mem_in=32, params=16 * 6,
            mem_n=1, mem_hi=4,
            x_sq=3, x_mean=3, x_sqrt=3, xn_ready=2,
            hi_T=26, yrows_ready=1,
            mk_mean=1, mk_sqrt=1, mk_n=1,
            zg_split=1, rawd_ready=1, qk_mean=1, qk_sqrt=1, knd_ready=1, qn_ready=1, blk_ready=1,
            hidrep=1, kc_mean=1, kc_sqrt=1, kcd_ready=1,
            sgw_ready=1, ln_mean=1, ln_sqrt=1, vn_ready=1, ob_ready=1,
            cs_ready=1, cs_exp=1, pc_ready=1,
            s_ready=len(UNITS), p_exp=len(UNITS), o_ready=1, merged_ready=2,
            xq_mean=1, xq_sqrt=1, xs_ready=len(XUNITS), xo_ready=1,
            cv_ready=1, w_exp=1, w_ready=1,
            u_out=KEYS, hot_ready=4 * S, g_full=2 * G_STEPS, g_out=2 * G_STEPS,
            eg_hi=KEYS, eg_ready=KEYS, v_out=1,
            acc_free0=sum(v == 0 for v in PARITY.values()), acc_free1=sum(v == 1 for v in PARITY.values()))
        PRIMED = dict(layer_free=2, u_out=4, g_out=2, acc_free0=1, acc_free1=1)
        sig = {n: Signal(sem(n), per, PRIMED.get(n, 0)) for n, per in PER.items()}
        n_uses = [sum(b == k for _, b in USES) for k in range(4)]
        filled = [Signal(sem(f"aux{b}_filled"), n_uses[b]) for b in range(4)]
        drained = [Signal(sem(f"aux{b}_drained"), n_uses[b], 1) for b in range(4)]
        turn, seen = {}, [0] * 4
        for name, b in USES:
            turn[name] = (b, seen[b])
            seen[b] += 1
        dve_step = sem("dve_step")
        act_step = sem("act_step")
        x_in = sem("x_in")
        const_in = sem("const_in")
        mem_sq, mem_mean, mem_sqrt = sem("mem_sq"), sem("mem_mean"), sem("mem_sqrt")
        zero_set = sem("zero_set")
        settled = sem("settled")
        out_done = sem("out_done")

        def bank(name):
            return aux[:, turn[name][0], :]

        class Engine:

            def __init__(self, eng, layer, own=None):
                self.e, self.layer, self.own, self.n, self.ahead = eng, layer, own, 0, 0

            def value(self, s, k):
                return s.value(self.layer, k + self.ahead * s.per)

            def wait(self, name, k=None):
                s = sig[name]
                self.e.wait_ge(s.sem, self.value(s, s.per if k is None else k))

            def wait_filled(self, use):
                b, j = turn[use]
                self.e.wait_ge(filled[b].sem, self.value(filled[b], j + 1))

            def wait_drained(self, use):
                b, j = turn[use]
                self.e.wait_ge(drained[b].sem, self.value(drained[b], j + 1))

            def wait_bank_free(self, use):
                b, j = turn[use]
                self.e.wait_ge(drained[b].sem, self.value(drained[b], j))

            def wait_block(self, block):
                i = BLOCKS.index(block)
                s = sig[f"acc_free{i % 2}"]
                self.e.wait_ge(s.sem, self.value(s, i // 2 + 1))

            def wait_pieces(self, n):
                self.e.wait_ge(used, self.layer * PIECES + (SLOTS + n))

            def settle(self):
                self.e.sem_inc(settled, 1)

            def step(self, ins, name=None, drains=None, block=None):
                if drains is not None:
                    b, j = turn[drains]
                    ins.then_inc(drained[b].sem, 1)
                    drained[b].sent += 1
                    self.wait_drained(drains)
                elif block is not None:
                    s = sig[f"acc_free{BLOCKS.index(block) % 2}"]
                    ins.then_inc(s.sem, 1)
                    s.sent += 1
                    self.wait_block(block)
                elif name is not None:
                    s = sig[name]
                    ins.then_inc(s.sem, 1)
                    s.sent += 1
                    self.e.wait_ge(s.sem, self.value(s, s.sent))
                else:
                    self.n += 1
                    ins.then_inc(self.own, 1)
                    self.e.wait_ge(self.own, self.n)

        def forget(count, *signals):
            for s in signals:
                s.sent -= count

        block = ctx.enter_context(nc.Block())

        @block.sync
        def _(sp):
            with sp.Fori(0, DEPTH * CHUNKS // RAW) as i:
                for r in range(RAW):
                    sp.wait_ge(lo_ready, i * (RAW * PER_CHUNK) + (r + 1) * PER_CHUNK)
                    sp.dma_start(raw[:, r], stream[bass.ds(i * RAW + r, 1)].rearrange(
                        "o p (k c) -> p (o k) c", c=COL)).then_inc(chunk_in[r], 16)
            sp.wait_ge(sig["layer_free"].sem, sig["layer_free"].value(DEPTH, 0))
            sp.dma_start(out.rearrange("(t p) d -> p t d", p=P), X[:]).then_inc(out_done, 16)
            sp.wait_ge(out_done, 16)

        @block.gpsimd
        def _(pool):
            pool.sem_inc(lo_ready, HELD)
            with pool.Fori(0, DEPTH) as layer:
                for first, end in ((0, SHARED), (SHARED, PIECES)):
                    with pool.Fori(0, (end - first) // HELD) as i:
                        for k in range(HELD):
                            if first == SHARED and k == HELD - 1:
                                pool.wait_ge(lo_shared, layer * ((PIECES - SHARED) // HELD) + i + 1)
                                pool.wait_ge(lo_ready, layer * PIECES + i * HELD + (HELD + first + k))
                                pool.sem_inc(lo_ready, 1)
                                continue
                            pool.wait_ge(hi_ready, layer * PIECES + i * HELD + (first + k + 1))
                            pool.wait_ge(used, layer * PIECES + i * HELD + (first + k + 1))
                            nc.gpsimd.tensor_tensor(w_lo[:, k % SLOTS, :], raw[:, k // PER_CHUNK, k % PER_CHUNK, :],
                                                    w_hi[:, k % SLOTS, :].bitcast(F32), ALU.subtract).then_inc(lo_ready, 1)

        @block.scalar
        def _(act):
            def load_memory(a, at):
                act.dma_start(memx, mem.rearrange("(t p) d -> p t d", p=P)).then_inc(sig["mem_in"].sem, 16)
                act.dma_start(col[:], cols[at].rearrange("o p c -> p (o c)")).then_inc(sig["mem_in"].sem, 16)

            def memory_hi(a, i):
                a.wait_filled(f"mem_T{i}")
                src = bank(f"mem_T{i}").rearrange("p (k t) -> p k t", t=S)
                for k in range(2):
                    kt = 2 * i + k
                    a.step(nc.scalar.activation(h_hi[:, kt, :], src[:, k, :], ACT.Copy,
                                                scale=col[:, C_MEM + kt:C_MEM + kt + 1]), "mem_hi" if k else None)

            first = Engine(act, 0, act_step)
            load_memory(first, slice(0, 1))
            act.dma_start(cst[:], consts).then_inc(const_in, 16)
            act.dma_start(X[:], x.rearrange("(t p) d -> p t d", p=P)).then_inc(x_in, 16)
            first.wait("mem_in")
            for t in range(T):
                nc.scalar.activation(junk[:, t, :], memx[:, t, :], ACT.Square, accum_out=ssm[:, t:t + 1]).then_inc(mem_sq, 1)
            act.wait_ge(mem_mean, 1)
            nc.scalar.activation(ssm, ssm, ACT.Sqrt).then_inc(mem_sqrt, 1)
            for i in range(4):
                memory_hi(first, i)
            act.sem_clear(act_step)
            forget(4, sig["mem_hi"])

            with act.Fori(0, DEPTH) as layer:
                a = Engine(act, layer, act_step)
                done = [0]

                PER_TURN = RAW * PER_CHUNK
                TURNS = CHUNKS // RAW * 16

                def hi_piece(k, turn_value, free_value):
                    act.wait_ge(chunk_in[(k // PER_CHUNK) % RAW], turn_value)
                    act.wait_ge(used, free_value)
                    nc.scalar.activation(w_hi[:, k % SLOTS, :], raw[:, (k // PER_CHUNK) % RAW, k % PER_CHUNK, :],
                                         ACT.Copy).then_inc(hi_ready, 1)

                def hi(n):
                    for _ in range(n):
                        k = done[0]
                        hi_piece(k, layer * TURNS + (k // PER_TURN + 1) * 16, layer * PIECES + (k + 1))
                        done[0] += 1
                        for m in range(5):
                            if done[0] == LAST[f"z_m{m}"] + SLOTS:
                                read_gates(m)

                def read_gates(m):
                    b = f"z_m{m}"
                    a.wait_pieces(LAST[b])
                    for t in range(T):
                        a.step(nc.scalar.activation(gates[:, t, m * COL:(m + 1) * COL], acc[:, PARITY[b] * 2 + t, :],
                                                    ACT.Tanh, scale=0.5), block=b if t == T - 1 else None)

                def hi_T(name, k0, nk, gain=1.0):
                    a.wait_filled(name)
                    src = bank(name).rearrange("p (k t) -> p k t", t=S)
                    for k in range(nk):
                        scale = gain if isinstance(gain, float) else col[:, gain + k:gain + k + 1]
                        a.step(nc.scalar.activation(rows_of(name[:2], k0)[0][:, k0 + k, :], src[:, k, :], ACT.Copy,
                                                    scale=scale), "hi_T" if k == nk - 1 else None)

                def half_squares(n):
                    for t in range(T):
                        a.step(nc.scalar.activation(junk[:, t, 0:COL], X[:, t, n * COL:(n + 1) * COL], ACT.Square,
                                                    accum_out=xsq[:, 2 * n + t:2 * n + t + 1]),
                               "x_sq" if n and t else None)

                def root(v, mean, done_name, k=1):
                    a.wait(mean, k)
                    a.step(nc.scalar.activation(v, v, ACT.Sqrt), done_name)

                hi(SLOTS)
                a.wait("layer_free", 0)
                for name, size, src in (("w1", 4256, parb), ("sgw", 1280, parr), ("zgw", 192, zgw)):
                    act.dma_start(big[:, OFF[name]:OFF[name] + size],
                                  src[bass.ds(layer, 1)].rearrange("o p c -> p (o c)")).then_inc(sig["params"].sem, 16)
                act.dma_start(lnr, lnrow[bass.ds(layer, 1)].broadcast_to((P, 512))).then_inc(sig["params"].sem, 16)
                act.dma_start(trl, tril).then_inc(sig["params"].sem, 16)
                act.dma_start(big[:, OFF["pm"]:OFF["pm"] + 1536], pm).then_inc(sig["params"].sem, 16)

                act.wait_ge(x_in, 16)
                for t in range(T):
                    a.step(nc.scalar.activation(junk[:, t, :], X[:, t, :], ACT.Square, accum_out=ssx[:, t:t + 1]),
                           "x_sq" if t else None)
                root(ssx, "x_mean", "x_sqrt", 1)
                hi(16)
                for i in range(4):
                    hi_T(f"mix_T{i}", 2 * i, 2, C_MIX + 2 * i)
                root(ssh[:, 0:8], "mk_mean", "mk_sqrt")
                hi(32)
                root(ssh, "qk_mean", "qk_sqrt")
                a.wait_pieces(LAST["z_sgu"])
                for t in range(T):
                    a.step(nc.scalar.activation(sg[:, t, :], acc[:, PARITY["z_sgu"] * 2 + t, :], ACT.Gelu_apprx_tanh),
                           block="z_sgu" if t == T - 1 else None)
                a.wait_filled("zg")
                a.step(nc.scalar.activation(ng, bank("zg")[:, 0:48].rearrange("p (t c) -> p t c", t=T), ACT.Tanh,
                                            scale=0.5),
                       drains="zg")
                hi(2)
                root(mvr[:, :, 1], "ln_mean", "ln_sqrt")
                hi(4)
                a.wait_filled("hid")
                a.step(nc.scalar.activation(hidT[:, :, :, 0:N_CMP], bank("hid")[:, 0:64].rearrange(
                    "p (c g n) -> p c g n", c=2, g=2)[:, :, :, 0:N_CMP], ACT.Gelu_apprx_tanh), drains="hid")
                hi(3)
                a.wait("kc_mean")
                a.step(nc.scalar.activation(ssk[0:32], ssk[0:32], ACT.Sqrt), "kc_sqrt")
                hi(7)
                a.wait("cs_ready")
                a.step(nc.scalar.activation(sc, sc, ACT.Exp), "cs_exp")
                for u, (t, br, j) in enumerate(UNITS):
                    w = P * (t + 1)
                    a.wait("s_ready", u + 1)
                    for h in range(2):
                        a.step(nc.scalar.activation(sring[:, u % 2, h, 0:w], sring[:, u % 2, h, 0:w], ACT.Exp,
                                                    bias=nmx[:, u % 2, h:h + 1],
                                                    accum_out=sums[:, (t * 2 + br) % 2, 2 * j + h:2 * j + h + 1]),
                               "p_exp" if h == 1 else None)
                    hi(2)
                hi_T("br_T2", 4, 2)
                for k in range(2):
                    a.step(nc.scalar.activation(h_hi[:, 6 + k, :], yT[:, k, :], ACT.Copy), "hi_T" if k else None)
                read_gates(5)
                hi(2)
                for i in range(2):
                    hi_T(f"br_T{i}", 2 * i, 2, 0.5)
                hi(10)
                for n in range(2):
                    for i in (2 * n, 2 * n + 1):
                        hi_T(f"mg_T{i}", 2 * i, 2, 0.5)
                    hi((4, 12)[n])
                for n in range(2):
                    for i in (2 * n, 2 * n + 1):
                        hi_T(f"xa_T{i}", 2 * i, 2, C_XA + 2 * i)
                    a.wait_block(f"out{n}")
                    half_squares(n)
                    if n == 0:
                        hi(4)
                root(ssx, "x_mean", "x_sqrt", 2)
                hi(8)
                root(ssh[:, 0:8], "xq_mean", "xq_sqrt")
                for u, (t, j) in enumerate(XUNITS):
                    a.wait("xs_ready", u + 1)
                    for h in range(2):
                        a.step(nc.scalar.activation(sring[:, u % 2, h, :], bank(f"xs{u}")[:, h * MEM:(h + 1) * MEM],
                                                    ACT.Exp, scale=ssh[:, 4 * t + 2 * j + h:4 * t + 2 * j + h + 1], bias=nmx[:, u % 2, h:h + 1],
                                                    accum_out=sums[:, t, 2 * j + h:2 * j + h + 1]),
                               **(dict(drains=f"xs{u}") if h else {}))
                for i in range(2):
                    hi_T(f"xo_T{i}", 2 * i, 2)
                hi(6)
                for n in range(2):
                    for i in (2 * n, 2 * n + 1):
                        hi_T(f"fu_T{i}", 2 * i, 2, C_FFN + 2 * i)
                    a.wait_block(f"xo{n}")
                    half_squares(n)
                    if n == 0:
                        hi(2)
                root(ssx, "x_mean", "x_sqrt", 3)
                for n in range(2):
                    hi(8)
                    for i in (2 * n, 2 * n + 1):
                        hi_T(f"ff_T{i}", 2 * i, 2, C_FFN + 2 * i)
                assert done[0] == PROJ + SLOTS
                def key_rows(i, key):
                    at = slice(key, key + 1) if isinstance(i, int) else bass.ds(i * 4 + key, 1)
                    return experts[:, at, :].rearrange("p o t -> p (o t)")

                def key_out(i, key):
                    act.wait_ge(used, layer * PIECES + i * 8 + (PROJ + SLOTS + 2 * (key + 1)))
                    nc.scalar.activation(key_rows(i, key), acc[:, key % 4, 0:S],
                                         ACT.Gelu_apprx_tanh).then_inc(sig["u_out"].sem, 1)

                for k0, k1 in ((0, EXP_AT), (EXP_AT, KEYS)):
                    a.step(nc.scalar.activation(tblw, tblw, ACT.Gelu_apprx_tanh))
                    if k0 == 0:
                        hi(2)
                    with act.Fori(0, (k1 - k0) // 4 - 1) as i:
                        for q in range(4):
                            key_out(i, k0 + q)
                            for r in range(2):
                                k = done[0] + 2 * q + r
                                hi_piece(k, layer * TURNS + i * 16 + (k // PER_TURN + 1) * 16,
                                         layer * PIECES + i * 8 + (k + 1))
                    done[0] += 2 * (k1 - k0) - 8
                    for q in range(4):
                        key_out(0, k1 - 4 + q)
                        if k1 == EXP_AT or q < 3:
                            hi(2)
                    if k1 == EXP_AT:
                        a.wait("cv_ready")
                        a.step(nc.scalar.activation(slot_w, slot_w, ACT.Exp), "w_exp")
                sig["u_out"].sent += KEYS

                def key_hi(i, key):
                    act.wait_ge(used, layer * PIECES + i * 8 + (SLOTS + PROJ + U_PIECES + 2 * (key - 1)))
                    nc.scalar.activation(eg[:, key % 2, 0, :], key_rows(i, key), ACT.Copy).then_inc(sig["eg_hi"].sem, 1)

                a.wait("g_out", G_STEPS)
                key_hi(0, 0)
                key_hi(0, 1)
                key = 2
                for end in (HALF, LOAD_AT) + tuple(k + 2 for k in MEM_AT) + (KEYS,):
                    steps = (end - key) // 4
                    with act.Fori(0, steps) as i:
                        for q in range(4):
                            for r in range(2):
                                k = done[0] + 2 * q + r
                                hi_piece(k, layer * TURNS + i * 16 + (k // PER_TURN + 1) * 16,
                                         layer * PIECES + i * 8 + (k + 1))
                                if r == 0:
                                    key_hi(i, key + q)
                    done[0] += 8 * steps
                    key += 4 * steps
                    while key < end:
                        hi(1)
                        key_hi(0, key)
                        hi(1)
                        key += 1
                    if end == HALF:
                        a.wait("g_out")
                        a.settle()
                    if end == LOAD_AT:
                        a.wait("eg_ready", HALF)
                        a.settle()
                        load_memory(a, bass.ds(layer + 1, 1))
                    if end - 2 in MEM_AT:
                        a.ahead = 1
                        memory_hi(a, MEM_AT.index(end - 2))
                        a.ahead = 0
                        a.settle()
                assert key == KEYS and done[0] == PIECES
                a.settle()
                act.sem_clear(act_step)

        @block.tensor
        def _(pe_):
            pe_.sem_inc(used, SLOTS)
            pe_.wait_ge(const_in, 16)

            def memory_T(e, i):
                e.wait("mem_n")
                e.wait_bank_free(f"mem_T{i}")
                for c in range(4):
                    k, t = 2 * i + c // 2, c % 2
                    ins = pe_.transpose(bank(f"mem_T{i}")[:, c * P:(c + 1) * P], memx[:, t, k * P:(k + 1) * P], ident)
                b, _ = turn[f"mem_T{i}"]
                ins.then_inc(filled[b].sem, 1)
                filled[b].sent += 1

            first = Engine(pe_, 0)
            for i in range(4):
                memory_T(first, i)
            forget(1, *filled)

            with pe_.Fori(0, DEPTH) as layer:
                e = Engine(pe_, layer)
                done = [0]
                waited = set()

                def fill(ins, use):
                    b, _ = turn[use]
                    ins.then_inc(filled[b].sem, 1)
                    filled[b].sent += 1

                def transposes(use, sources, waited=False):
                    if not waited:
                        e.wait_bank_free(use)
                    at = 0
                    for src in sources:
                        rows = src.shape[0]
                        ins = pe_.transpose(bank(use)[:, at:at + rows], src, ident[0:rows, 0:rows])
                        at += rows
                    fill(ins, use)

                def rows_T(uses, src, k0=0):
                    for i, use in enumerate(uses):
                        transposes(use, [src[:, t, k * P:(k + 1) * P] for k in (k0 + 2 * i, k0 + 2 * i + 1)
                                         for t in range(T)])

                piece_block = [(b, k, LAST[b] - FIRST[b]) for b in BLOCKS for k in range(pieces_of(b))]
                def rows_there(tag, kt):
                    if (tag, kt // 2) not in waited:
                        waited.add((tag, kt // 2))
                        if (tag, kt) == ("br", 6):
                            e.wait("yrows_ready")
                        else:
                            e.wait_drained(f"{tag}_T{kt // 2}")

                def take(n):
                    for _ in range(n):
                        b, k, depth = piece_block[done[0]]
                        if k == 0:
                            i = BLOCKS.index(b)
                            s = sig[f"acc_free{i % 2}"]
                            pe_.wait_ge(s.sem, s.value(layer, i // 2))
                        pe_.wait_ge(lo_ready, layer * PIECES + (HELD + done[0] + 1))
                        slot = done[0] % SLOTS
                        tag, first = ROWS.get(b.rstrip("01"), ("mix", 0))
                        kt = first + k
                        rows_there(tag, kt)
                        r_hi, r_lo = rows_of(tag, kt)
                        for t in range(T):
                            dst = acc[:, PARITY[b] * 2 + t, :]
                            ts = slice(t * P, (t + 1) * P)
                            pe_.matmul(dst, r_hi[:, kt, ts], w_hi[:, slot, :], start=(k == 0), stop=False)
                            pe_.matmul(dst, r_hi[:, kt, ts], w_lo[:, slot, :], start=False, stop=False)
                            ins = pe_.matmul(dst, r_lo[:, kt, ts], w_hi[:, slot, :], start=False, stop=(k == depth - 1))
                        ins.then_inc(used, 1)
                        done[0] += 1

                for n in range(T):
                    e.wait("layer_free", n - 1)
                    take(8)
                e.wait("xn_ready", 1)
                rows_T([f"mix_T{i}" for i in range(4)], xn)
                take(16)
                e.wait("mk_n")
                for i in range(2):
                    transposes(f"mk_T{i}", [mk[:, t, h * XD:(h + 1) * XD] for h in (2 * i, 2 * i + 1) for t in range(T)])
                take(16)
                e.wait("zg_split")
                e.wait_bank_free("zg")
                for t in range(T):
                    for k in range(KD):
                        ts = slice(t * P, (t + 1) * P)
                        dst = bank("zg")[:, t * 24:(t + 1) * 24]
                        pe_.matmul(dst, h_hi[:, k, ts], zg_hi[:, k, :], start=(k == 0), stop=False)
                        pe_.matmul(dst, h_hi[:, k, ts], zg_lo[:, k, :], start=False, stop=False)
                        ins = pe_.matmul(dst, h_lo[:, k, ts], zg_hi[:, k, :], start=False, stop=(k == KD - 1))
                fill(ins, "zg")
                e.wait("rawd_ready")
                for i in range(2):
                    transposes(f"raw_T{i}", [rawd[:, t, cg, :, :] for cg in (2 * i, 2 * i + 1) for t in range(T)])
                e.wait("knd_ready")
                for br in range(2):
                    transposes(f"kn_T{br}", [knd[:, t, br, g, :, :] for g in range(KVG) for t in range(T)])
                take(3)
                e.wait("qn_ready")
                for i in range(2):
                    transposes(f"q_T{i}", [zq[:, t, j * P:(j + 1) * P] for j in (2 * i, 2 * i + 1) for t in range(T)])
                take(3)
                e.wait("params")
                e.wait("blk_ready")
                e.wait_bank_free("hid")
                for c in range(2):
                    for lp in range(L_CMP // 2):
                        ins = pe_.matmul(bank("hid")[:, c * 32:(c + 1) * 32], w1[:, c, lp, :],
                                         blk[:, c, lp, :, :], start=(lp == 0), stop=(lp == L_CMP // 2 - 1))
                fill(ins, "hid")
                for t in range(T):
                    use = f"pool_d{t}"
                    e.wait_bank_free(use)
                    for g in range(4):
                        dst = bank(use)[0:DK, g * P:(g + 1) * P]
                        chans = slice(g * DK, (g + 1) * DK)
                        ins = pe_.matmul(dst, zp[:, t, chans], pmx[:, t, g, :], start=True, stop=(t == 0))
                        if t:
                            ins = pe_.matmul(dst, zp[:, 0, chans], pmx[:, 2, g, :], start=False, stop=True)
                    fill(ins, use)
                take(3)
                e.wait_drained("hid")
                e.wait_bank_free("cmp_k")
                fill(pe_.matmul(bank("cmp_k")[0:32, 0:DK], hidT[:, 0, :, :], w2[:, 0, :],
                                start=True, stop=True), "cmp_k")
                e.wait("hidrep")
                e.wait_bank_free("cmp_v")
                fill(pe_.matmul(bank("cmp_v")[:, 0:DK], hid_rep, w2[:, 1, :], start=True, stop=True), "cmp_v")
                take(3)
                e.wait("sgw_ready")
                e.wait("vn_ready")
                e.wait_bank_free("mixed")
                for t in range(T):
                    for g in range(SGU_G):
                        at = t * SGU_W + g * 64
                        ins = pe_.matmul(bank("mixed")[:, at:at + 64], sgw[:, g, :], vn[:, t, g * 64:(g + 1) * 64],
                                         start=True, stop=True)
                fill(ins, "mixed")
                e.wait_drained("pool_d1")
                e.wait_bank_free("pool_y")
                for m in range(2):
                    for t in range(T):
                        for g in (2 * m, 2 * m + 1):
                            at = m * S + t * P
                            ins = pe_.matmul(bank("pool_y")[:, at:at + P], pw[0:DK, g, :], dT[0:DK, t, g, :],
                                             start=(g % 2 == 0), stop=(g % 2 == 1))
                fill(ins, "pool_y")
                take(2)
                e.wait("kcd_ready")
                e.wait_bank_free("kc_T")
                e.settle()
                transposes("kc_T", [kcd[0:32]], waited=True)
                take(2)
                e.wait_drained("q_T1")
                e.wait_drained("kc_T")
                e.wait_bank_free("cmp_s")
                for t in range(T):
                    for j in range(PAIRS):
                        at = t * P + j * 32
                        ins = pe_.matmul(bank("cmp_s")[:, at:at + 32], qT[:, j, t * P:(t + 1) * P], KcB[:, j // 2, :, :],
                                         start=True, stop=True)
                fill(ins, "cmp_s")

                def scores(u):
                    t, br, j = UNITS[u]
                    w = P * (t + 1)
                    e.wait_bank_free(f"s{u}")
                    fill(pe_.matmul(bank(f"s{u}")[:, 0:2 * w], qT[:, j, t * P:(t + 1) * P], kTm[:, br, j // 2, :, 0:w],
                                    start=True, stop=True), f"s{u}")

                e.wait_drained("kn_T1")
                scores(0)
                scores(1)
                for u, (t, br, j) in enumerate(UNITS):
                    take(1)
                    e.wait("p_exp", u + 1)
                    transposes(f"p_T{u}", [sring[:, u % 2, h, c * P:(c + 1) * P] for h in range(2) for c in range(t + 1)])
                    if u + 2 < len(UNITS):
                        scores(u + 2)
                    take(1)
                    if u == len(UNITS) - 1:
                        rows_T(["br_T2"], ob)
                    e.wait_drained(f"p_T{u}")
                    use = f"o{u // PAIRS}"
                    if j == 0:
                        e.wait_bank_free(use)
                    for h in range(2):
                        for c in range(t + 1):
                            at = (2 * j + h) * DK
                            g = j // 2
                            ins = pe_.matmul(bank(use)[:, at:at + DK], pT[:, u % 2, h * (t + 1) + c, :],
                                             zkv[:, c, 3 + 2 * br, g * DK:(g + 1) * DK], start=(c == 0), stop=(c == t))
                    if j == PAIRS - 1:
                        fill(ins, use)
                    if u == 1:
                        e.wait("pc_ready")
                        transposes("pc_T", [sc[:, t, :, :] for t in range(T)])
                    if u in (2, 3):
                        e.wait_drained("pc_T")
                        e.wait_drained("cmp_v")
                        e.wait_bank_free(f"oc{u - 2}")
                        fill(pe_.matmul(bank(f"oc{u - 2}"), pcT[:, u - 2, :], vblk, start=True, stop=True), f"oc{u - 2}")
                take(2)
                e.wait("o_ready")
                rows_T(["br_T0", "br_T1"], ot)
                take(10)
                for n in range(2):
                    e.wait("merged_ready", n + 1)
                    rows_T([f"mg_T{i}" for i in (2 * n, 2 * n + 1)], merged, 4 * n)
                    take((4, 12)[n])
                for n in range(2):
                    e.wait_block(f"out{n}")
                    rows_T([f"xa_T{i}" for i in (2 * n, 2 * n + 1)], X, 4 * n)
                    take((4, 8)[n])
                e.wait_block("xq")
                for i in range(2):
                    transposes(f"xq_T{i}", [xqt[:, t, h * XD:(h + 1) * XD] for h in (2 * i, 2 * i + 1) for t in range(T)])

                def xscores(u):
                    t, j = XUNITS[u]
                    e.wait_bank_free(f"xs{u}")
                    for h in range(2):
                        ins = pe_.matmul(bank(f"xs{u}")[:, h * MEM:(h + 1) * MEM], xqT[:, 2 * j + h, t * P:(t + 1) * P],
                                         mkT[:, 2 * j + h, :], start=True, stop=True)
                    fill(ins, f"xs{u}")

                e.wait_drained("xq_T1")
                e.wait_block("mem_v")
                xscores(0)
                xscores(1)
                for u, (t, j) in enumerate(XUNITS):
                    e.wait_drained(f"xs{u}")
                    transposes(f"xp_T{u}", [sring[:, u % 2, h, c * P:(c + 1) * P] for h in range(2) for c in range(2)])
                    if u + 2 < len(XUNITS):
                        xscores(u + 2)
                    e.wait_drained(f"xp_T{u}")
                    use = f"xo_{t}"
                    if j == 0:
                        e.wait_bank_free(use)
                    for h in range(2):
                        for c in range(2):
                            at = (2 * j + h) * XD
                            ins = pe_.matmul(bank(use)[:, at:at + XD], pT[:, u % 2, h * 2 + c, :],
                                             mv[:, c, at:at + XD], start=(c == 0), stop=(c == 1))
                    if j == 1:
                        fill(ins, use)
                e.wait("xo_ready")
                rows_T(["xo_T0", "xo_T1"], xo)
                take(6)
                for n in range(2):
                    e.wait_block(f"xo{n}")
                    rows_T([f"fu_T{i}" for i in (2 * n, 2 * n + 1)], X, 4 * n)
                    take((2, 8)[n])
                e.wait("xn_ready", 2)
                rows_T(["ff_T0", "ff_T1"], xn)
                take(8)
                rows_T(["ff_T2", "ff_T3"], xn, 4)
                e.wait_block("pq0")
                e.wait_block("pq1")
                rows_T([f"pq_T{i}" for i in range(4)], pq)
                for i in range(4):
                    e.wait_drained(f"pq_T{i}")
                for t in range(T):
                    for i in range(4):
                        use = f"ps{t}_{i}"
                        e.wait_bank_free(use)
                        for h in range(2):
                            ins = pe_.matmul(bank(use)[:, h * 256:(h + 1) * 256], pqT[:, 2 * i + h, t * P:(t + 1) * P],
                                             keys, start=True, stop=True)
                        fill(ins, use)
                def weights_step(i, s, half):
                    pe_.wait_ge(sig["g_out"].sem, layer * (2 * G_STEPS) + i * 4 + (half * G_STEPS + s + 1))
                    pe_.wait_ge(sig["hot_ready"].sem, layer * (4 * S) + i * (8 * G_TOK)
                                + (half * 2 * S + 2 * G_TOK * (s + 1)))
                    for r in range(G_TOK):
                        for c in range(PARTS):
                            at = KEYS + c * HALF
                            ins = pe_.matmul(aux[:, s % 2, r * HALF:(r + 1) * HALF], hots[:, s % 2, r, 0:KEYS],
                                             hots[:, s % 2, r, at:at + HALF], start=(c == 0), stop=(c == PARTS - 1))
                    ins.then_inc(sig["g_full"].sem, 1)

                for kt in range(KD):
                    rows_there("ff", kt)
                e.settle()
                for k0, k1 in ((0, SLOTS_AT), (SLOTS_AT, HALF), (HALF, KEYS)):
                    if k0 == SLOTS_AT:
                        e.wait("w_ready")
                        transposes("slot_T0", [ab[:, w, t, :, :] for w in range(2) for t in range(T)])
                        transposes("slot_T1", [cv[:, t, :, :] for t in range(T)])
                        e.settle()
                    if k0 == HALF:
                        for b in range(4):
                            pe_.wait_ge(drained[b].sem, drained[b].value(layer, drained[b].per))
                        e.settle()
                    with pe_.Fori(0, (k1 - k0) // 4) as i:
                        for r in range(8):
                            q, kh = r // 2, r % 2
                            if kh == 0:
                                if k0 == HALF:
                                    weights_step(i, q, 0)
                                pe_.wait_ge(sig["u_out"].sem, layer * KEYS + i * 4 + (k0 + q + 1))
                            pe_.wait_ge(lo_ready, layer * PIECES + i * 8 + (HELD + PROJ + 2 * k0 + r + 1))
                            for k in range(4):
                                kt = kh * 4 + k
                                wh = w_hi[:, r % SLOTS, k * P:(k + 1) * P]
                                pe_.matmul(acc[:, q, 0:S], wh, h_hi[:, kt, :], start=(kt == 0), stop=False)
                                pe_.matmul(acc[:, q, 0:S], wh, h_lo[:, kt, :], start=False, stop=False)
                                ins = pe_.matmul(acc[:, q, 0:S], w_lo[:, r % SLOTS, k * P:(k + 1) * P], h_hi[:, kt, :],
                                                 start=False, stop=(kt == KD - 1))
                            ins.then_inc(used, 1)
                pe_.wait_ge(zero_set, 1)
                pe_.wait_ge(sig["u_out"].sem, layer * KEYS + (KEYS + 4))
                for q in range(4):
                    pe_.matmul(acc[:, q, :], zeros[:], zeros[:, 0:1].broadcast_to((P, COL)), start=True, stop=False)
                for k0, k1 in zip((0, HALF) + MEM_AT, (HALF,) + MEM_AT + (KEYS,)):
                    if k0 in MEM_AT:
                        e.ahead = 1
                        memory_T(e, MEM_AT.index(k0))
                        e.ahead = 0
                    with pe_.Fori(0, (k1 - k0) // 4) as i:
                        for r in range(8):
                            q, dh = r // 2, r % 2
                            if dh == 0:
                                if k0 == 0:
                                    weights_step(i, q, 1)
                                pe_.wait_ge(sig["eg_ready"].sem, layer * KEYS + i * 4 + (k0 + q + 1))
                            pe_.wait_ge(lo_ready, layer * PIECES + i * 8 + (HELD + PROJ + U_PIECES + 2 * k0 + r + 1))
                            slot = r % SLOTS
                            for t in range(T):
                                ts = slice(t * P, (t + 1) * P)
                                dst = acc[:, 2 * t + dh, :]
                                pe_.matmul(dst, eg[:, q % 2, 0, ts], w_hi[:, slot, :], start=False, stop=False)
                                pe_.matmul(dst, eg[:, q % 2, 0, ts], w_lo[:, slot, :], start=False, stop=False)
                                ins = pe_.matmul(dst, eg[:, q % 2, 1, ts], w_hi[:, slot, :], start=False, stop=False)
                            ins.then_inc(used, 1)
                for q in range(4):
                    ins = pe_.matmul(acc[:, q, :], zeros[:], zeros[:, 0:1].broadcast_to((P, COL)), start=False, stop=True)
                ins.then_inc(sig["v_out"].sem, 1)

        @block.vector
        def _(dve):
            V = nc.vector
            V.memset(zeros[:], 0.0).then_inc(zero_set, 1)
            dve.wait_ge(const_in, 16)
            V.tensor_copy(iota_b[:], iota).then_inc(zero_set, 1)
            dve.wait_ge(zero_set, 2)
            for n, v in PRIMED.items():
                if n != "layer_free":
                    dve.sem_inc(sig[n].sem, v)
            for d in drained:
                dve.sem_inc(d.sem, 1)
            dve.sem_inc(sig["layer_free"].sem, PRIMED["layer_free"])

            def memory_rows(d):
                d.wait("mem_in")
                for t in range(T):
                    d.step(V.tensor_scalar(memx[:, t, :], memx[:, t, :], ssm[:, t:t + 1], None, ALU.mult),
                           "mem_n" if t else None)

            def memory_lo(d, i):
                d.wait("mem_hi", i + 1)
                src = bank(f"mem_T{i}").rearrange("p (k t) -> p k t", t=S)
                for k in range(2):
                    kt = 2 * i + k
                    ins = V.scalar_tensor_tensor(out=h_lo[:, kt, :], in0=src[:, k, :], scalar=col[:, C_MEM + kt:C_MEM + kt + 1],
                                                 in1=h_hi[:, kt, :].bitcast(F32), op0=ALU.mult, op1=ALU.subtract)
                    if k:
                        d.step(ins, drains=f"mem_T{i}")
                    else:
                        d.step(ins)

            first = Engine(dve, 0, dve_step)
            dve.wait_ge(mem_sq, T)
            first.step(V.tensor_scalar(ssm, ssm, 1.0 / D, EPS, ALU.mult, ALU.add))
            dve.sem_inc(mem_mean, 1)
            dve.wait_ge(mem_sqrt, 1)
            first.step(V.reciprocal(ssm, ssm))
            memory_rows(first)
            for i in range(4):
                memory_lo(first, i)
            dve.sem_clear(dve_step)
            forget(1, sig["mem_n"], *drained)
            dve.wait_ge(x_in, 16)

            with dve.Fori(0, DEPTH) as layer:
                d = Engine(dve, layer, dve_step)
                hiT = [0]

                def stt(o, i0, s, i1, op0, op1):
                    return V.scalar_tensor_tensor(out=o, in0=i0, scalar=s, in1=i1, op0=op0, op1=op1)

                def lo_T(name, k0, nk, gain=1.0, src=None):
                    hiT[0] += 1
                    d.wait("hi_T", hiT[0])
                    r_hi, r_lo = rows_of(name[:2], k0)
                    if src is None:
                        src = bank(name).rearrange("p (k t) -> p k t", t=S)
                    for k in range(nk):
                        dst, hi = r_lo[:, k0 + k, :], r_hi[:, k0 + k, :].bitcast(F32)
                        g = gain if isinstance(gain, float) else col[:, gain + k:gain + k + 1]
                        ins = stt(dst, src[:, k, :], g, hi, ALU.mult, ALU.subtract)
                        if k < nk - 1:
                            d.step(ins)
                        elif name in turn:
                            d.step(ins, drains=name)
                        else:
                            d.step(ins, name)

                def mean(v, n, name):
                    d.step(V.tensor_scalar(v, v, 1.0 / n, EPS, ALU.mult, ALU.add), name)

                def rows_norm(v, src, dst, name):
                    for t in range(T):
                        d.step(V.tensor_scalar(dst[:, t, :], src[:, t, :], v[:, t:t + 1], None, ALU.mult),
                               name if t == T - 1 else None)

                def read_block(b, dsts, scale=None):
                    d.wait_pieces(LAST[b])
                    n = len(dsts)
                    for i, (t, c0, c1, dst) in enumerate(dsts):
                        src = acc[:, PARITY[b] * 2 + t, c0:c1]
                        ins = V.tensor_copy(dst, src) if scale is None else \
                            V.tensor_scalar(dst, src, scale[:, t:t + 1], None, ALU.mult)
                        d.step(ins, block=b if i == n - 1 else None)

                d.wait("x_sq", 1)
                mean(ssx, D, "x_mean")
                d.wait("x_sqrt", 1)
                d.step(V.reciprocal(ssx, ssx))
                rows_norm(ssx, X, xn, "xn_ready")
                d.wait("params")
                zgf = zg_hi[:, :, :].bitcast(F32)
                d.step(V.tensor_copy(zg_hi[:, :, :], zgr))
                d.step(V.tensor_tensor(zg_lo[:, :, :], zgr, zgf, ALU.subtract), "zg_split")
                for br in range(2):
                    for h in range(2):
                        d.step(V.memset(kTm[(1 - h) * DK:(2 - h) * DK, br, :, h, :], 0.0))
                d.step(V.memset(hid_rep, 0.0))
                d.step(V.memset(hidT, 0.0))
                d.step(V.memset(KcB, 0.0))
                d.step(V.memset(blk, 0.0))
                d.step(V.tensor_tensor(sgw, sgw, trl.unsqueeze(1).broadcast_to((P, SGU_G, P)), ALU.mult), "sgw_ready")
                read_block("mem_k", [(t, 0, COL, mk[:, t, :]) for t in range(T)])
                read_block("mem_v", [(t, 0, COL, mv[:, t, :]) for t in range(T)])
                for i in range(4):
                    lo_T(f"mix_T{i}", 2 * i, 2, C_MIX + 2 * i)
                mkh = mk.rearrange("p t (h c) -> p (t h) c", c=XD)
                tmph = tmp.rearrange("p t (h c) -> p (t h) c", c=XD)
                d.step(V.tensor_tensor(tmph, mkh, mkh, ALU.mult))
                d.step(V.tensor_reduce(ssh[:, 0:8], tmph, AX.X, ALU.add))
                mean(ssh[:, 0:8], XD, "mk_mean")
                d.wait("mk_sqrt")
                d.step(V.reciprocal(ssh[:, 0:8], ssh[:, 0:8]))
                d.step(V.tensor_tensor(mkh, mkh, ssh[:, 0:8].unsqueeze(2).broadcast_to((P, 8, XD)), ALU.mult), "mk_n")
                zkf = zkv.rearrange("p t c d -> p t (c d)")
                read_block("z_q", [(t, 0, COL, zq[:, t, :]) for t in range(T)])
                read_block("z_kv0", [(t, 0, COL, zkf[:, t, 0:COL]) for t in range(T)])
                for i in range(2):
                    d.wait_filled(f"mk_T{i}")
                    d.step(V.tensor_scalar(mkT[:, 2 * i:2 * i + 2, :], bank(f"mk_T{i}").rearrange("p (h m) -> p h m", h=2),
                                           col[:, C_XKN:C_XKN + 1], None, ALU.mult), drains=f"mk_T{i}")
                read_block("z_kv1", [(t, 0, 256, zkf[:, t, COL:768]) for t in range(T)]
                           + [(t, 256, COL, zp[:, t, :]) for t in range(T)])
                for t in range(T):
                    src = zkv[:, t, 0:2, :].rearrange("p c (g d) -> p (c g) d", g=2).unsqueeze(2).broadcast_to((P, 4, 2, DK))
                    d.step(V.tensor_copy(rawd[:, t], src), "rawd_ready" if t else None)
                zqh = zq.rearrange("p t (h c) -> p (t h) c", c=DK)
                tq = tmp.rearrange("p t (h c) -> p (t h) c", c=DK)
                d.step(V.tensor_tensor(tq, zqh, zqh, ALU.mult))
                d.step(V.tensor_reduce(ssh[:, 0:16], tq, AX.X, ALU.add))
                for br in range(2):
                    kk = zkv[:, :, 2 + 2 * br, :].rearrange("p t (g c) -> p t g c", g=2)
                    tk = tmp[:, 0, 0:256].rearrange("p (t g c) -> p t g c", t=2, g=2)
                    d.step(V.tensor_tensor(tk, kk, kk, ALU.mult))
                    d.step(V.tensor_reduce(ssh[:, 16 + 4 * br:20 + 4 * br].rearrange("p (t g) -> p t g", t=2), tk,
                                           AX.X, ALU.add))
                mean(ssh, DK, "qk_mean")
                d.wait("qk_sqrt")
                d.step(V.reciprocal(ssh, ssh))
                for t in range(T):
                    for br in range(2):
                        r = ssh[:, 16 + 4 * br + 2 * t:18 + 4 * br + 2 * t].unsqueeze(2).unsqueeze(3).broadcast_to((P, 2, 2, DK))
                        src = zkv[:, t, 2 + 2 * br, :].rearrange("p (g c) -> p g c", g=2).unsqueeze(2).broadcast_to((P, 2, 2, DK))
                        d.step(V.tensor_tensor(knd[:, t, br], src, r, ALU.mult), "knd_ready" if t and br else None)
                d.step(V.tensor_tensor(zqh, zqh, ssh[:, 0:16].unsqueeze(2).broadcast_to((P, 16, DK)), ALU.mult), "qn_ready")
                d.wait_block("z_sgu")
                for t in range(T):
                    d.step(V.bn_stats(bns[:, t, :], sg[:, t, SGU_W:2 * SGU_W]))
                    d.step(V.bn_aggr(mvr[:, t, :], bns[:, t, :]))
                d.step(V.tensor_scalar(mvr[:, :, 1], mvr[:, :, 1], 1.0, EPS, ALU.mult, ALU.add), "ln_mean")
                for i in range(2):
                    use = f"raw_T{i}"
                    d.wait_filled(use)
                    v = bank(use).rearrange("p (c s) -> p c s", c=2)
                    d.step(V.tensor_copy(KV2[0:DK, 2 * i:2 * i + 2, :], v[0:DK]))
                    d.step(V.tensor_copy(KV2[DK:P, 2 * i:2 * i + 2, 0:S - 1], v[DK:P, :, 1:S]), drains=use)
                k2 = KV2.rearrange("p c (n l r) -> p l c n r", l=8, r=2)
                for c in range(2):
                    for lh in range(2):
                        for g in range(KVG):
                            src = k2[:, :, 2 * c + g, lh:lh + N_CMP, 0]
                            add = pe[:, c, 8 * lh:8 * lh + 8].unsqueeze(2).broadcast_to((P, 8, N_CMP))
                            d.step(V.tensor_tensor(blk[:, c, 8 * lh:8 * lh + 8, g, 0:N_CMP], src, add, ALU.add),
                                   "blk_ready" if c and lh and g else None)
                for br in range(2):
                    use = f"kn_T{br}"
                    d.wait_filled(use)
                    v = bank(use).rearrange("p (g s) -> p g s", g=2)
                    for h in range(2):
                        ps = slice(h * DK, (h + 1) * DK)
                        ins = V.tensor_scalar(kTm[ps, br, :, h, :], v[ps], col[ps, C_KN + 1 + br:C_KN + 2 + br], None, ALU.mult)
                        if h:
                            d.step(ins, drains=use)
                        else:
                            d.step(ins)
                for i in range(2):
                    use = f"q_T{i}"
                    d.wait_filled(use)
                    d.step(V.tensor_scalar(qT[:, 2 * i:2 * i + 2, :], bank(use).rearrange("p (j s) -> p j s", j=2),
                                           col[:, C_QN:C_QN + 1], None, ALU.mult), drains=use)
                d.wait("ln_sqrt")
                d.step(V.reciprocal(mvr[:, :, 1], mvr[:, :, 1]))
                for t in range(T):
                    d.step(V.tensor_scalar(vn[:, t, :], sg[:, t, SGU_W:2 * SGU_W], mvr[:, t, 0:1], mvr[:, t, 1:2],
                                           ALU.subtract, ALU.mult))
                    d.step(V.tensor_tensor(vn[:, t, :], vn[:, t, :], lnr[:, 0:256], ALU.mult))
                    d.step(V.tensor_tensor(vn[:, t, :], vn[:, t, :], lnr[:, 256:512], ALU.add), "vn_ready" if t else None)
                d.wait_drained("hid")
                d.step(V.tensor_copy(hid_rep[:, :, :, 0:N_CMP],
                                     hidT[:, 1, :, 0:N_CMP].unsqueeze(2).broadcast_to((P, 2, 4, N_CMP))), "hidrep")
                for t in range(T):
                    use = f"pool_d{t}"
                    d.wait_filled(use)
                    d.step(V.tensor_copy(dT[0:DK, t], bank(use)[0:DK].rearrange("p (g s) -> p g s", g=4)), drains=use)
                d.wait_filled("cmp_k")
                d.step(V.tensor_copy(kcs[0:32], bank("cmp_k")[0:32, 0:DK]), drains="cmp_k")
                d.step(V.tensor_tensor(kcq[0:32], kcs[0:32], kcs[0:32], ALU.mult))
                d.step(V.tensor_reduce(ssk[0:32], kcq[0:32], AX.X, ALU.add))
                mean(ssk[0:32], DK, "kc_mean")
                d.wait_filled("cmp_v")
                d.step(V.tensor_tensor(vblk.rearrange("p (h c) -> p h c", h=8),
                                       bank("cmp_v")[:, 0:DK].unsqueeze(1).broadcast_to((P, 8, DK)),
                                       bmask.unsqueeze(2).broadcast_to((P, 8, DK)), ALU.mult), drains="cmp_v")
                d.wait("kc_sqrt")
                d.step(V.reciprocal(ssk[0:32], ssk[0:32]))
                d.step(V.tensor_scalar(kcd[0:32], kcs[0:32].unsqueeze(1).broadcast_to((32, 2, DK)), ssk[0:32], None, ALU.mult),
                       "kcd_ready")
                d.wait_filled("mixed")
                for t in range(T):
                    for g in range(SGU_G):
                        cs = slice(g * 64, (g + 1) * 64)
                        at = t * SGU_W + g * 64
                        ins = stt(ob[:, t, cs], bank("mixed")[:, at:at + 64], col[:, C_SB + g:C_SB + g + 1], sg[:, t, cs],
                                  ALU.add, ALU.mult)
                        if t == T - 1 and g == SGU_G - 1:
                            d.step(ins, drains="mixed")
                        else:
                            d.step(ins)
                sig["ob_ready"].sent += 1
                dve.sem_inc(sig["ob_ready"].sem, 1)
                d.wait_filled("pool_y")
                for m in range(2):
                    ins = V.tensor_scalar(yT[:, m, :], bank("pool_y")[:, m * S:(m + 1) * S],
                                          col[:, C_PSC + m:C_PSC + m + 1], None, ALU.mult)
                    if m:
                        d.step(ins, drains="pool_y")
                    else:
                        d.step(ins)
                d.wait_filled("kc_T")
                kct = bank("kc_T")[:, 0:32].rearrange("p (g n) -> p g n", g=2)
                for h in range(2):
                    ps = slice(h * DK, (h + 1) * DK)
                    ins = V.tensor_scalar(KcB[ps, :, h, 0:N_CMP], kct[ps, :, 0:N_CMP], col[ps, C_KN:C_KN + 1], None, ALU.mult)
                    if h:
                        d.step(ins, drains="kc_T")
                    else:
                        d.step(ins)
                d.wait_filled("cmp_s")
                for t in range(T):
                    ins = stt(sc[:, t], bank("cmp_s")[:, t * P:(t + 1) * P].rearrange("p (h n) -> p h n", h=8), DK ** -0.5,
                              cneg[:, t, :].unsqueeze(1).broadcast_to((P, 8, 16)), ALU.mult, ALU.add)
                    if t:
                        d.step(ins, drains="cmp_s")
                    else:
                        d.step(ins)
                scf = sc.rearrange("p t h n -> p (t h) n")
                cmb = cmx.unsqueeze(2).broadcast_to((P, 16, 16))
                d.step(V.tensor_reduce(cmx, scf, AX.X, ALU.max))
                d.step(V.tensor_tensor(scf, scf, cmb, ALU.subtract), "cs_ready")

                def unit_scores(u):
                    t, br, j = UNITS[u]
                    w = P * (t + 1)
                    use = f"s{u}"
                    mask = (cmask[:, P:2 * P] if t == 0 else cmask).unsqueeze(1).broadcast_to((P, 2, w))
                    d.wait_filled(use)
                    d.step(stt(sring[:, u % 2, :, 0:w], bank(use)[:, 0:2 * w].rearrange("p (h s) -> p h s", h=2), DK ** -0.5,
                               mask, ALU.mult, ALU.add), drains=use)
                    d.step(V.tensor_reduce(nmx[:, u % 2, :], sring[:, u % 2, :, 0:w], AX.X, ALU.max, negate=True), "s_ready")

                def combine(use, t, k, weights, first, done=None):
                    d.step(V.reciprocal(coef, weights))
                    d.step(stt(coef, ng[:, t, k:24:3], 1.0, coef, ALU.add, ALU.mult))
                    d.wait_filled(use)
                    dst = (ot if first else tmp)[:, t, :].rearrange("p (h c) -> p h c", h=8)
                    d.step(V.tensor_tensor(dst, bank(use).rearrange("p (h c) -> p h c", h=8),
                                           coef.unsqueeze(2).broadcast_to((P, 8, DK)), ALU.mult), drains=use)
                    if not first:
                        d.step(V.tensor_tensor(ot[:, t, :], ot[:, t, :], tmp[:, t, :], ALU.add), done)

                unit_scores(0)
                unit_scores(1)
                d.wait("cs_exp")
                d.step(V.tensor_tensor(sc, sc, cone.unsqueeze(2).broadcast_to((P, 2, 8, 16)), ALU.mult))
                d.step(V.tensor_reduce(cmx, scf, AX.X, ALU.add))
                d.step(V.tensor_scalar(cmx, cmx, 1e-30, None, ALU.max), "pc_ready")
                d.wait_drained("zg")
                for u, (t, br, j) in enumerate(UNITS):
                    use = f"p_T{u}"
                    d.wait_filled(use)
                    n = 2 * (t + 1)
                    d.step(V.tensor_copy(pT[:, u % 2, 0:n, :], bank(use)[:, 0:n * P].rearrange("p (n s) -> p n s", n=n)), drains=use)
                    if u + 2 < len(UNITS):
                        unit_scores(u + 2)
                    if u == 1:
                        d.wait_filled("pc_T")
                        d.step(V.tensor_copy(pcT, bank("pc_T")[:, 0:256].rearrange("p (t s) -> p t s", t=2)), drains="pc_T")
                    if u in (2, 3):
                        combine(f"oc{u - 2}", u - 2, 0, cmx[:, (u - 2) * 8:(u - 1) * 8], True)
                    if u == len(UNITS) - 1:
                        lo_T("br_T2", 4, 2)
                        lo_T("yrows_ready", 6, 2, src=yT)
                    if j == PAIRS - 1:
                        combine(f"o{u // PAIRS}", t, 1 + br, sums[:, (t * 2 + br) % 2, :], False,
                                "o_ready" if u == len(UNITS) - 1 else None)
                d.wait_block("z_m4")
                d.wait_block("z_m5")

                def gate(branch, n, first):
                    b = f"lift_{'abc'[branch]}{n}"
                    d.wait_pieces(LAST[b])
                    gs = slice(branch * D + n * COL, branch * D + (n + 1) * COL)
                    cs = slice(n * COL, (n + 1) * COL)
                    for t in range(T):
                        dst = merged[:, t, cs] if first else tmp[:, t, :]
                        d.step(stt(dst, gates[:, t, gs], 1.0, acc[:, PARITY[b] * 2 + t, :], ALU.add, ALU.mult),
                               block=b if t else None)
                    if not first:
                        d.step(V.tensor_tensor(merged[:, :, cs], merged[:, :, cs], tmp, ALU.add),
                               "merged_ready" if branch == 0 else None)

                gate(1, 0, True)
                for i in range(2):
                    lo_T(f"br_T{i}", 2 * i, 2, 0.5)
                gate(2, 0, False)
                gate(0, 0, False)
                gate(1, 1, True)
                for i in range(2):
                    lo_T(f"mg_T{i}", 2 * i, 2, 0.5)
                gate(2, 1, False)
                gate(0, 1, False)
                for i in range(2, 4):
                    lo_T(f"mg_T{i}", 2 * i, 2, 0.5)

                def add_block(b, n):
                    d.wait_pieces(LAST[b])
                    for t in range(T):
                        v = X[:, t, n * COL:(n + 1) * COL]
                        d.step(V.tensor_tensor(v, v, acc[:, PARITY[b] * 2 + t, :], ALU.add), block=b if t else None)

                def add_rows(block, tag, gain, k):
                    for n in range(2):
                        add_block(f"{block}{n}", n)
                        for i in (2 * n, 2 * n + 1):
                            lo_T(f"{tag}_T{i}", 2 * i, 2, gain + 2 * i)
                    d.wait("x_sq", k)
                    d.step(V.tensor_tensor(ssx, xsq[:, 0:2], xsq[:, 2:4], ALU.add))
                    mean(ssx, D, "x_mean")
                    d.wait("x_sqrt", k)
                    d.step(V.reciprocal(ssx, ssx))

                add_rows("out", "xa", C_XA, 2)
                read_block("xq", [(t, 0, COL, xqt[:, t, :]) for t in range(T)], ssx)
                xqh = xqt.rearrange("p t (h c) -> p (t h) c", c=XD)
                d.step(V.tensor_tensor(tmph, xqh, xqh, ALU.mult))
                d.step(V.tensor_reduce(ssh[:, 0:8], tmph, AX.X, ALU.add))
                mean(ssh[:, 0:8], XD, "xq_mean")
                d.wait("xq_sqrt")
                for i in range(2):
                    use = f"xq_T{i}"
                    d.wait_filled(use)
                    d.step(V.tensor_scalar(xqT[:, 2 * i:2 * i + 2, :], bank(use).rearrange("p (j s) -> p j s", j=2),
                                           col[:, C_XQN:C_XQN + 1], None, ALU.mult), drains=use)

                d.wait("xq_sqrt")
                d.step(V.reciprocal(ssh[:, 0:8], ssh[:, 0:8]))
                d.step(V.tensor_scalar(ssh[:, 0:8], ssh[:, 0:8], XD ** -0.5, None, ALU.mult))

                def x_scores(u):
                    t, j = XUNITS[u]
                    d.wait_filled(f"xs{u}")
                    m = nmx[:, u % 2, :]
                    d.step(V.tensor_reduce(m, bank(f"xs{u}").rearrange("p (h m) -> p h m", h=2), AX.X, ALU.max, negate=True))
                    d.step(V.tensor_tensor(m, m, ssh[:, 4 * t + 2 * j:4 * t + 2 * j + 2], ALU.mult), "xs_ready")

                x_scores(0)
                x_scores(1)
                for u, (t, j) in enumerate(XUNITS):
                    use = f"xp_T{u}"
                    d.wait_filled(use)
                    d.step(V.tensor_copy(pT[:, u % 2], bank(use).rearrange("p (n s) -> p n s", n=4)), drains=use)
                    if u + 2 < len(XUNITS):
                        x_scores(u + 2)
                    if j == 1:
                        d.wait_drained(f"xs{u}")
                        d.step(V.reciprocal(coef[:, 0:4], sums[:, t, 0:4]))
                        d.wait_filled(f"xo_{t}")
                        d.step(V.tensor_tensor(xo[:, t, :].rearrange("p (h c) -> p h c", h=4),
                                               bank(f"xo_{t}").rearrange("p (h c) -> p h c", h=4),
                                               coef[:, 0:4].unsqueeze(2).broadcast_to((P, 4, XD)), ALU.mult),
                               drains=f"xo_{t}")
                sig["xo_ready"].sent += 1
                dve.sem_inc(sig["xo_ready"].sem, 1)
                for i in range(2):
                    lo_T(f"xo_T{i}", 2 * i, 2)
                add_rows("xo", "fu", C_FFN, 3)
                rows_norm(ssx, X, xn, "xn_ready")
                for n in range(2):
                    read_block(f"pq{n}", [(t, 0, COL, pq[:, t, n * COL:(n + 1) * COL]) for t in range(T)], ssx)
                    for i in (2 * n, 2 * n + 1):
                        lo_T(f"ff_T{i}", 2 * i, 2, C_FFN + 2 * i)
                for i in range(4):
                    use = f"pq_T{i}"
                    d.wait_filled(use)
                    d.step(V.tensor_copy(pqT[:, 2 * i:2 * i + 2, :], bank(use).rearrange("p (j s) -> p j s", j=2)), drains=use)
                for t in range(T):
                    for i in range(4):
                        use = f"ps{t}_{i}"
                        d.wait_filled(use)
                        d.step(V.tensor_copy(rs[:, 2 * i:2 * i + 2], bank(use).rearrange("p (h f k) -> p h f k", h=2, f=2)),
                               drains=use)
                    for h in range(PH):
                        for f in range(2):
                            v = rs[:, h, f, :]
                            d.settle()
                            d.step(V.max(tv[:, h, f, 0:8], v))
                            d.step(V.max_index(ti[:, h, f, 0:8], tv[:, h, f, 0:8], v))
                            d.step(V.match_replace(v, tv[:, h, f, 0:8], v, LOWEST))
                            d.step(V.max(tv[:, h, f, 8:16], v))
                            d.step(V.max_index(ti[:, h, f, 8:16], tv[:, h, f, 8:16], v))
                    d.step(V.tensor_copy(topf[:], topi[:]))
                    for h in range(PH):
                        d.step(V.tensor_tensor(cand[:, h], tv[:, h, 0, :].unsqueeze(2).broadcast_to((P, 16, 16)),
                                               tv[:, h, 1, :].unsqueeze(1).broadcast_to((P, 16, 16)), ALU.add))
                    for h in range(PH):
                        v = cand[:, h].rearrange("p i j -> p (i j)")
                        c = ci[:, h * 16:(h + 1) * 16]
                        w = cv[:, t, h, :]
                        d.step(V.max(w[:, 0:8], v))
                        d.step(V.max_index(c[:, 0:8], w[:, 0:8], v))
                        d.step(V.match_replace(v, w[:, 0:8], v, LOWEST))
                        d.step(V.max(w[:, 8:16], v))
                        d.step(V.max_index(c[:, 8:16], w[:, 8:16], v))
                    d.step(V.tensor_scalar(cia, ci, 4, None, ALU.logical_shift_right))
                    d.step(V.tensor_copy(iab[:, 0, :], cia))
                    d.step(V.tensor_scalar(cia, ci, 15, None, ALU.bitwise_and))
                    d.step(V.tensor_copy(iab[:, 1, :], cia))
                    for f in range(2):
                        d.step(V.tensor_tensor(onehot, iab[:, f, :].unsqueeze(2).broadcast_to((P, 128, 16)),
                                               iota16.unsqueeze(1).broadcast_to((P, 128, 16)), ALU.is_equal))
                        oh = onehot.rearrange("p (h k) j -> p h k j", h=PH)
                        d.step(V.tensor_tensor(oh, oh, tf[:, :, f, :].unsqueeze(2).broadcast_to((P, PH, 16, 16)), ALU.mult))
                        d.step(V.tensor_reduce(ab[:, f, t].rearrange("p h k -> p (h k)"), onehot, AX.X, ALU.add))
                cvf = cv[:, :, :, :].rearrange("p t h k -> p (t h) k")
                d.step(V.tensor_reduce(cmx, cvf, AX.X, ALU.max))
                d.step(V.tensor_tensor(cvf, cvf, cmb, ALU.subtract), "cv_ready")
                d.wait("w_exp")
                d.step(V.tensor_reduce(cmx, cvf, AX.X, ALU.add))
                d.step(V.reciprocal(cmx, cmx))
                d.step(V.tensor_tensor(cvf, cvf, cmb, ALU.mult), "w_ready")
                d.wait_filled("slot_T0")
                d.step(V.tensor_copy(slot_a[:], bank("slot_T0")[:, 0:S]))
                d.step(V.tensor_copy(slot_b[:], bank("slot_T0")[:, S:2 * S]), drains="slot_T0")
                d.wait_filled("slot_T1")
                d.step(V.tensor_copy(slot_w, bank("slot_T1")[:, 0:S]), drains="slot_T1")
                for c in range(PARTS):
                    d.step(V.tensor_copy(slot_parts[:, c, :], slot_w))
                    if c < PARTS - 1:
                        d.step(V.tensor_tensor(slot_w, slot_w, slot_parts[:, c, :], ALU.subtract))

                def one_hots(i, s, half):
                    for r in range(G_TOK):
                        t = i * (4 * G_TOK) + (s * G_TOK + r)
                        one = lambda v: v[:, bass.ds(t, 1)]
                        V.tensor_scalar(hots[:, s % 2, r, 0:KEYS], iota_b[:], one(slot_b), None,
                                        ALU.is_equal).then_inc(sig["hot_ready"].sem, 1)
                        stt(hots[:, s % 2, r, KEYS:HOT].rearrange("p (c a) -> p c a", c=PARTS),
                            iota_b[:, half * HALF:(half + 1) * HALF].unsqueeze(1).broadcast_to((P, PARTS, HALF)), one(slot_a),
                            slot_parts[:, :, bass.ds(t, 1)].broadcast_to((P, PARTS, HALF)),
                            ALU.is_equal, ALU.mult).then_inc(sig["hot_ready"].sem, 1)

                def weigh(i, s, half):
                    dve.wait_ge(sig["g_full"].sem, layer * (2 * G_STEPS) + i * 4 + (half * G_STEPS + s + 1))
                    v = experts[:, half * HALF:(half + 1) * HALF, bass.ds(i * (4 * G_TOK) + s * G_TOK, G_TOK)]
                    v = v.rearrange("p a t -> p t a")
                    V.tensor_tensor(v, v, aux[:, s % 2, 0:G_TOK * HALF].rearrange("p (t a) -> p t a", t=G_TOK),
                                    ALU.mult).then_inc(sig["g_out"].sem, 1)

                def weighted(i, q):
                    src = experts[:, bass.ds(i * 4 + q, 1), :].rearrange("p o t -> p (o t)")
                    dve.wait_ge(sig["eg_hi"].sem, layer * KEYS + i * 4 + (q + 1))
                    V.tensor_tensor(eg[:, q % 2, 1, :], src, eg[:, q % 2, 0, :].bitcast(F32),
                                    ALU.subtract).then_inc(sig["eg_ready"].sem, 1)

                one_hots(0, 0, 0)
                one_hots(0, 1, 0)
                d.wait("u_out", HALF)
                d.settle()
                with dve.Fori(0, G_STEPS // 4 - 1) as i:
                    for q in range(4):
                        weigh(i, q, 0)
                        one_hots(i, q + 2, 0)
                last = G_STEPS // 4 - 1
                for q in range(4):
                    weigh(last, q, 0)
                    if q < 2:
                        one_hots(last, q + 2, 0)
                    else:
                        one_hots(0, q - 2, 1)
                d.wait("g_out", G_STEPS)
                weighted(0, 0)
                d.wait("u_out", KEYS)
                d.settle()
                with dve.Fori(0, G_STEPS // 4 - 1) as i:
                    for q in range(4):
                        weigh(i, q, 1)
                        weighted(i, q + 1)
                        one_hots(i, q + 2, 1)
                for q in range(4):
                    weigh(last, q, 1)
                    if q < 3:
                        weighted(last, q + 1)
                    if q < 2:
                        one_hots(last, q + 2, 1)
                sig["hot_ready"].sent += 4 * S
                sig["g_out"].sent += 2 * G_STEPS
                d.wait("g_out")
                lo_at = tuple(k + 4 for k in MEM_AT)
                for k0, k1 in zip((HALF, NORM_AT) + lo_at, (NORM_AT,) + lo_at + (KEYS,)):
                    d.ahead = 1
                    if k0 == NORM_AT:
                        memory_rows(d)
                    if k0 in lo_at:
                        memory_lo(d, lo_at.index(k0))
                    d.ahead = 0
                    d.settle()
                    with dve.Fori(k0 // 4, k1 // 4) as i:
                        for q in range(4):
                            weighted(i, q)
                        dve.wait_ge(hi_ready, layer * PIECES + i * HELD + (PROJ + U_PIECES + HELD))
                        dve.wait_ge(used, layer * PIECES + i * HELD + (PROJ + U_PIECES + HELD))
                        V.tensor_tensor(w_lo[:, SLOTS - 1, :], raw[:, RAW - 1, PER_CHUNK - 1, :],
                                        w_hi[:, SLOTS - 1, :].bitcast(F32), ALU.subtract).then_inc(lo_shared, 1)
                d.wait("eg_ready")
                d.wait("v_out")
                for t in range(T):
                    d.step(V.tensor_tensor(X[:, t, :].rearrange("p (n c) -> p n c", n=2),
                                           X[:, t, :].rearrange("p (n c) -> p n c", n=2),
                                           acc[:, 2 * t:2 * t + 2, :], ALU.add), "layer_free")
                d.settle()
                dve.sem_clear(dve_step)
        for n in ("x_sq", "hi_T", "s_ready", "xs_ready", "merged_ready", "p_exp", "acc_free0", "acc_free1", "g_out", "xn_ready"):
            assert sig[n].sent == sig[n].per, (n, sig[n].sent, sig[n].per)
        for s in filled + drained:
            assert s.sent == s.per, ([f.sent for f in filled], [f.sent for f in drained], n_uses)


def constants():
    c = np.zeros((P, K_END), np.float32)
    r = np.arange(P)
    c[:, K_ID:K_ID + P] = np.eye(P)
    c[:, K_IO:K_IO + P] = r[None, :]
    c[:, K_CM + P:K_CM + 2 * P] = np.where(r[None, :] <= r[:, None], 0.0, NEG)
    end = np.arange(NP_) * D_CMP + L_CMP - 1
    for t in range(T):
        ok = (end[None, :] <= (t * P + r)[:, None]) & (np.arange(NP_) < N_CMP)[None, :]
        c[:, K_CN + t * NP_:K_CN + (t + 1) * NP_] = np.where(ok, 0.0, NEG)
        c[:, K_C1 + t * NP_:K_C1 + (t + 1) * NP_] = ok
    c[:, K_BM:K_BM + HEADS] = (r[:, None] // NP_) == np.arange(HEADS)[None, :]
    c[:, K_I16:K_I16 + TOPK] = np.arange(TOPK)[None, :]
    tril = (r[:, None] <= r[None, :]).astype(np.float32)
    pm = np.zeros((3, len(WINDOWS), S // T, P), np.float32)
    for g, w in enumerate(WINDOWS):
        m = np.zeros((S, S), np.float32)
        for t in range(S):
            m[max(0, t - w + 1):t + 1, t] = np.float32(1.0) / min(t + 1, w)
            m[t, t] -= 1.0
        pm[0, g], pm[1, g], pm[2, g] = m[:P, :P], m[P:, P:], m[:P, P:]
    return c, tril, np.ascontiguousarray(pm.transpose(2, 0, 1, 3)).reshape(P, -1)


def layouts(inp):
    def proj(w, n):
        return w[:, n * COL:(n + 1) * COL].reshape(-1, P, COL)

    stream = np.empty((DEPTH, PIECES, P, COL), np.float32)
    for l in range(DEPTH):
        w_in = inp["w_in"][l]
        q0, kv0, g0 = 0, 512, 512 + 768
        sg0 = g0 + 24
        p0, m0 = sg0 + 512, sg0 + 512 + 256
        z = [w_in[:, q0:kv0], w_in[:, kv0:kv0 + 512], np.concatenate([w_in[:, kv0 + 512:g0], w_in[:, p0:m0]], 1),
             w_in[:, sg0:p0]] + [w_in[:, m0 + i * 512:m0 + (i + 1) * 512] for i in range(6)]
        parts = [proj(inp["xa_wk"][l], 0), proj(inp["xa_wv"][l], 0)] + [proj(w, 0) for w in z]
        for n in range(2):
            parts += [proj(inp[k][l], n) for k in ("lift_b", "lift_c", "lift_a")]
        parts += [proj(inp["w_out"][l], n) for n in range(2)] + [proj(inp["xa_wq"][l], 0)]
        parts += [proj(inp["xa_wo"][l], n) for n in range(2)] + [proj(inp["peer_wq"][l], n) for n in range(2)]
        stream[l, :PROJ] = np.concatenate(parts)
        u = inp["peer_u"][l].reshape(KEYS, KEYS, 2, 4, P).transpose(0, 2, 4, 3, 1)
        stream[l, PROJ:PROJ + U_PIECES] = u.reshape(U_PIECES, P, COL)
        v = inp["peer_v"][l].reshape(KEYS, KEYS, 2, COL).transpose(0, 2, 1, 3)
        stream[l, PROJ + U_PIECES:] = v.reshape(V_PIECES, P, COL)
    stream = stream.reshape(DEPTH * CHUNKS, PER_CHUNK, P, COL).transpose(0, 2, 1, 3).reshape(DEPTH * CHUNKS, P, -1)

    cols = np.zeros((DEPTH + 1, P, C_END), np.float32)
    for name, c in (("mix_norm", C_MIX), ("xa_norm", C_XA), ("ffn_norm", C_FFN), ("mem_norm", C_MEM)):
        cols[:DEPTH, :, c:c + KD] = inp[name].reshape(DEPTH, KD, P).transpose(0, 2, 1)
    cols[:DEPTH, :, C_QN] = np.tile(inp["nsa_q_norm"], (1, 2))
    cols[:DEPTH, :, C_KN:C_KN + 3] = np.tile(inp["nsa_k_norm"], (1, 1, 2)).transpose(0, 2, 1)
    cols[:DEPTH, :, C_XQN], cols[:DEPTH, :, C_XKN] = inp["xa_q_norm"], inp["xa_k_norm"]
    cols[:DEPTH, :, C_PSC:C_PSC + 2] = inp["pool_scale"].reshape(DEPTH, 2, P).transpose(0, 2, 1)
    cols[:DEPTH, :, C_SB:C_SB + 4] = inp["sgu_b"].transpose(0, 2, 1)

    w1 = inp["cmp_w1"].reshape(DEPTH, 2, 16, 2, DK, CMP_HID).transpose(0, 3, 4, 1, 2, 5).reshape(DEPTH, P, -1)
    w2 = inp["cmp_w2"].transpose(0, 2, 1, 3).reshape(DEPTH, P, -1)
    pe = inp["cmp_pe"].reshape(DEPTH, 2, 16, 2, DK).transpose(0, 3, 4, 1, 2).reshape(DEPTH, P, -1)
    parb = np.concatenate([w1, w2, pe], 2)
    sgw = inp["sgu_w"].transpose(0, 3, 1, 2).reshape(DEPTH, P, -1)
    pw = np.zeros((DEPTH, P, 4, 2, DK), np.float32)
    for g in range(4):
        pw[:, :DK, g, g % 2, :] = inp["pool_w"][:, g]
    keys = np.zeros((DEPTH, 2, DK, 2, KEYS), np.float32)
    keys[:, 0, :, 0], keys[:, 1, :, 1] = (inp[k].transpose(0, 2, 1) for k in ("peer_keys1", "peer_keys2"))
    parr = np.concatenate([sgw, pw.reshape(DEPTH, P, -1), keys.reshape(DEPTH, P, -1)], 2)
    lnrow = np.concatenate([inp["sgu_ln_g"], inp["sgu_ln_b"]], 1)
    zgw = inp["w_in"][:, :, 1280:1304].reshape(DEPTH, KD, P, 24).transpose(0, 2, 1, 3).reshape(DEPTH, P, -1)
    consts, tril, pm = constants()
    arrays = dict(x=inp["x"][0], mem=inp["mem"][0], stream=stream, cols=cols, parb=parb, parr=parr, lnrow=lnrow,
                  zgw=zgw, consts=consts, pm=pm, tril=tril)
    return {k: np.ascontiguousarray(v) for k, v in arrays.items()}


_INS = ["x", "mem", "stream", "cols", "parb", "parr", "lnrow", "zgw", "consts", "pm", "tril"]


def kernel(**inputs):
    import concourse.bacc as _bacc
    from concourse.bass_utils import run_bass_kernel_spmd as _run

    arrays = layouts({k: np.asarray(v) for k, v in inputs.items()})
    nc = _bacc.Bacc("TRN2", target_bir_lowering=False, num_devices=1)
    aps = {k: nc.dram_tensor(k + "_dram", arrays[k].shape, mybir.dt.float32, kind="ExternalInput").ap() for k in _INS}
    out = nc.dram_tensor("out_dram", (S, D), mybir.dt.float32, kind="ExternalOutput").ap()
    trunk(nc, out=out, **aps)
    r = _run(nc, [{k + "_dram": arrays[k] for k in _INS}], core_ids=[0])
    return r.results[0]["out_dram"].reshape(1, S, D)
```
